# Optimizing a Trainium2 kernel written in Bass

```python
import numpy as np
import jax
import jax.numpy as jnp
from jax import lax
import jax, jax.numpy as jnp

D_MODEL = 1024
BATCH = 1
SEQ = 256
DEPTH = 1

HEAD_DIM = 64
NSA_HEADS = D_MODEL // (2 * HEAD_DIM)
NSA_KV_GROUPS = max(1, NSA_HEADS // 4)
NSA_HPG = NSA_HEADS // NSA_KV_GROUPS
NSA_CMP_LEN = 32
NSA_CMP_STRIDE = 16
NSA_CMP_HID = 128
NSA_SEL_BLOCK = 64
NSA_SEL_TOP = 16
NSA_WINDOW = 512
NSA_Q_CHUNK = 64
MOBA_HEADS = D_MODEL // (2 * HEAD_DIM)
MOBA_BLOCK = 256
MOBA_TOP = 3
MOBA_Q_CHUNK = 32
N_EXPERTS = 32
TOP_K = 4
D_FF = 1024
SWIGLU_LIMIT = 7.0
SWIGLU_ALPHA = 1.702
MOE_BLOCK = 128
EPS = 1e-6
NEG = -1e30
FORCE_SCORE = 1e4

NSA_W = NSA_HEADS * HEAD_DIM
NSA_KV_W = NSA_KV_GROUPS * HEAD_DIM
MOBA_W = MOBA_HEADS * HEAD_DIM
MIX_W = NSA_W + MOBA_W
IN_WIDTHS = (NSA_W, NSA_KV_W, NSA_KV_W, NSA_KV_W, NSA_KV_W, NSA_KV_W, NSA_KV_W,
             3 * NSA_HEADS, MOBA_W, MOBA_W, MOBA_W)
IN_W = sum(IN_WIDTHS)


def rms_norm(x, g):
    xf = x.astype(jnp.float32)
    y = xf * lax.rsqrt(jnp.mean(xf * xf, axis=-1, keepdims=True) + EPS)
    return (y * g.astype(jnp.float32)).astype(x.dtype)

def alibi_slopes(n):
    return jnp.asarray(2.0 ** (-8.0 * np.arange(1, n + 1) / n), dtype=jnp.float32)

def masked_softmax(s, mask):
    s = jnp.where(mask, s.astype(jnp.float32), NEG)
    p = jax.nn.softmax(s, axis=-1)
    return jnp.where(mask, p, 0.0)

def _heads(t, n_heads):
    b, s, _ = t.shape
    return t.reshape(b, s, n_heads, HEAD_DIM).transpose(0, 2, 1, 3)

_gather_blocks = jax.vmap(jax.vmap(lambda blocks, idx: blocks[idx]))

def _compress(kv, pos, w1, w2):
    s = kv.shape[2]
    n_cmp = (s - NSA_CMP_LEN) // NSA_CMP_STRIDE + 1
    idx = NSA_CMP_STRIDE * np.arange(n_cmp)[:, None] + np.arange(NSA_CMP_LEN)[None, :]
    blocks = kv[:, :, idx] + pos
    flat = blocks.reshape(kv.shape[0], kv.shape[1], n_cmp, NSA_CMP_LEN * HEAD_DIM)
    return jax.nn.gelu(flat @ w1) @ w2

def nsa_mixer(q, k_cmp, v_cmp, k_slc, v_slc, k_win, v_win, gates, k_gain, cmp_pos, cmp_w1, cmp_w2):
    B, G, Hg, S, dh = q.shape
    scale = dh ** -0.5
    sl = alibi_slopes(G * Hg).reshape(1, G, Hg, 1, 1)
    kc = rms_norm(_compress(k_cmp, cmp_pos[0], cmp_w1[0], cmp_w2[0]), k_gain)
    vc = _compress(v_cmp, cmp_pos[1], cmp_w1[1], cmp_w2[1])
    n_cmp = kc.shape[2]
    cmp_start = NSA_CMP_STRIDE * np.arange(n_cmp)
    cmp_end = jnp.asarray(cmp_start + NSA_CMP_LEN - 1, dtype=jnp.int32)
    cmp_center = jnp.asarray(cmp_start + 0.5 * (NSA_CMP_LEN - 1), dtype=jnp.float32)
    n_sel = S // NSA_SEL_BLOCK
    sel_start = NSA_SEL_BLOCK * np.arange(n_sel)
    incid = jnp.asarray((cmp_start[:, None] <= sel_start[None, :] + NSA_SEL_BLOCK - 1)
                        & (cmp_start[:, None] + NSA_CMP_LEN - 1 >= sel_start[None, :]), dtype=jnp.float32)
    n_top = min(NSA_SEL_TOP, n_sel)
    ks = rms_norm(k_slc, k_gain).reshape(B, G, n_sel, NSA_SEL_BLOCK, dh)
    vs = v_slc.reshape(B, G, n_sel, NSA_SEL_BLOCK, dh)
    pad = ((0, 0), (0, 0), (NSA_WINDOW, 0), (0, 0))
    kw = jnp.pad(rms_norm(k_win, k_gain), pad)
    vw = jnp.pad(v_win, pad)
    blk_ids = jnp.arange(n_sel)[None, :]
    in_blk = jnp.arange(NSA_SEL_BLOCK)
    win_off = jnp.arange(NSA_WINDOW + NSA_Q_CHUNK)
    C = NSA_Q_CHUNK
    m_sel = n_top * NSA_SEL_BLOCK

    def chunk(q0):
        qc = lax.dynamic_slice_in_dim(q, q0, C, axis=3)
        gc = lax.dynamic_slice_in_dim(gates, q0, C, axis=3)
        t = q0 + jnp.arange(C)
        tf = t.astype(jnp.float32)
        s = jnp.einsum('bghcd,bgnd->bghcn', qc, kc, preferred_element_type=jnp.float32) * scale
        s = s - sl * (tf[:, None] - cmp_center[None, :])
        p_cmp = masked_softmax(s, cmp_end[None, :] <= t[:, None])
        o_cmp = jnp.einsum('bghcn,bgnd->bghcd', p_cmp.astype(vc.dtype), vc)
        imp = jnp.einsum('bghcn,nj->bgcj', p_cmp, incid)
        cur = (t // NSA_SEL_BLOCK)[:, None]
        forced = (blk_ids == 0) | (blk_ids == cur) | (blk_ids == cur - 1)
        imp = jnp.where(forced, FORCE_SCORE, imp)
        imp = jnp.where(blk_ids <= cur, imp, NEG)
        _, sel = lax.top_k(imp, n_top)
        ksel = _gather_blocks(ks, sel).reshape(B, G, C, m_sel, dh)
        vsel = _gather_blocks(vs, sel).reshape(B, G, C, m_sel, dh)
        pos = (sel[..., None] * NSA_SEL_BLOCK + in_blk).reshape(B, G, C, m_sel)
        dist = (t[None, None, :, None] - pos)[:, :, None]
        s = jnp.einsum('bghcd,bgcmd->bghcm', qc, ksel, preferred_element_type=jnp.float32) * scale
        s = s - sl * dist.astype(jnp.float32)
        p = masked_softmax(s, dist >= 0)
        o_sel = jnp.einsum('bghcm,bgcmd->bghcd', p.astype(vsel.dtype), vsel)
        kwc = lax.dynamic_slice_in_dim(kw, q0, NSA_WINDOW + C, axis=2)
        vwc = lax.dynamic_slice_in_dim(vw, q0, NSA_WINDOW + C, axis=2)
        pos_w = q0 - NSA_WINDOW + win_off
        dist_w = t[:, None] - pos_w[None, :]
        mask_w = (dist_w >= 0) & (dist_w < NSA_WINDOW) & (pos_w >= 0)[None, :]
        s = jnp.einsum('bghcd,bgkd->bghck', qc, kwc, preferred_element_type=jnp.float32) * scale
        s = s - sl * dist_w.astype(jnp.float32)
        p = masked_softmax(s, mask_w)
        o_win = jnp.einsum('bghck,bgkd->bghcd', p.astype(vwc.dtype), vwc)
        return gc[..., 0:1] * o_cmp + gc[..., 1:2] * o_sel + gc[..., 2:3] * o_win

    out = lax.map(chunk, jnp.arange(0, S, C))
    return out.transpose(1, 0, 4, 2, 3, 5).reshape(B, S, G * Hg * dh)

def moba_mixer(q, k, v):
    B, H, S, dh = q.shape
    scale = dh ** -0.5
    sl = alibi_slopes(H).reshape(1, H, 1, 1)
    n_blk = -(-S // MOBA_BLOCK)
    pad = ((0, 0), (0, 0), (0, n_blk * MOBA_BLOCK - S), (0, 0))
    kp = jnp.pad(k, pad)
    vp = jnp.pad(v, pad)
    kb = kp.reshape(B, H, n_blk, MOBA_BLOCK, dh)
    vb = vp.reshape(B, H, n_blk, MOBA_BLOCK, dh)
    kmean = jnp.mean(kb.astype(jnp.float32), axis=3)
    n_top = min(MOBA_TOP, n_blk - 1)
    in_blk = jnp.arange(MOBA_BLOCK)
    blk_ids = jnp.arange(n_blk)
    C = MOBA_Q_CHUNK
    m_g = n_top * MOBA_BLOCK

    def chunk(q0):
        qc = lax.dynamic_slice_in_dim(q, q0, C, axis=2)
        t = q0 + jnp.arange(C)
        cb = q0 // MOBA_BLOCK
        kcur = lax.dynamic_slice_in_dim(kp, cb * MOBA_BLOCK, MOBA_BLOCK, axis=2)
        vcur = lax.dynamic_slice_in_dim(vp, cb * MOBA_BLOCK, MOBA_BLOCK, axis=2)
        dist_c = t[:, None] - (cb * MOBA_BLOCK + in_blk)[None, :]
        s_c = jnp.einsum('bhcd,bhkd->bhck', qc, kcur, preferred_element_type=jnp.float32) * scale
        s_c = s_c - sl * dist_c.astype(jnp.float32)
        mask_c = jnp.broadcast_to(dist_c >= 0, s_c.shape)
        if n_top > 0:
            gate = jnp.einsum('bhcd,bhnd->bhcn', qc, kmean, preferred_element_type=jnp.float32)
            gate = jnp.where(blk_ids < cb, gate, NEG)
            _, sel = lax.top_k(gate, n_top)
            kg = _gather_blocks(kb, sel).reshape(B, H, C, m_g, dh)
            vg = _gather_blocks(vb, sel).reshape(B, H, C, m_g, dh)
            pos_g = (sel[..., None] * MOBA_BLOCK + in_blk).reshape(B, H, C, m_g)
            dist_g = t[None, None, :, None] - pos_g
            s_g = jnp.einsum('bhcd,bhcmd->bhcm', qc, kg, preferred_element_type=jnp.float32) * scale
            s_g = s_g - sl * dist_g.astype(jnp.float32)
            mask_g = jnp.repeat(sel < cb, MOBA_BLOCK, axis=-1)
            p = masked_softmax(jnp.concatenate([s_g, s_c], axis=-1),
                               jnp.concatenate([mask_g, mask_c], axis=-1))
            o = (jnp.einsum('bhcm,bhcmd->bhcd', p[..., :m_g].astype(vg.dtype), vg)
                 + jnp.einsum('bhck,bhkd->bhcd', p[..., m_g:].astype(vcur.dtype), vcur))
        else:
            p = masked_softmax(s_c, mask_c)
            o = jnp.einsum('bhck,bhkd->bhcd', p.astype(vcur.dtype), vcur)
        return o

    out = lax.map(chunk, jnp.arange(0, S, C))
    return out.transpose(1, 0, 3, 2, 4).reshape(B, S, H * dh)

def hybrid_mixer(h, w_in, w_out, nsa_q_gain, nsa_k_gain, cmp_pos, cmp_w1, cmp_w2, moba_q_gain, moba_k_gain):
    B, S, _ = h.shape
    z = h @ w_in
    points = [int(v) for v in np.cumsum(IN_WIDTHS)[:-1]]
    q_n, kc, vc, ks, vs, kw, vw, g_n, q_m, k_m, v_m = jnp.split(z, points, axis=-1)
    qn = rms_norm(_heads(q_n, NSA_HEADS), nsa_q_gain).reshape(B, NSA_KV_GROUPS, NSA_HPG, S, HEAD_DIM)
    gates = jax.nn.sigmoid(g_n.reshape(B, S, NSA_KV_GROUPS, NSA_HPG, 3)).transpose(0, 2, 3, 1, 4)
    o_nsa = nsa_mixer(qn, _heads(kc, NSA_KV_GROUPS), _heads(vc, NSA_KV_GROUPS),
                      _heads(ks, NSA_KV_GROUPS), _heads(vs, NSA_KV_GROUPS),
                      _heads(kw, NSA_KV_GROUPS), _heads(vw, NSA_KV_GROUPS),
                      gates, nsa_k_gain, cmp_pos, cmp_w1, cmp_w2)
    o_moba = moba_mixer(rms_norm(_heads(q_m, MOBA_HEADS), moba_q_gain),
                        rms_norm(_heads(k_m, MOBA_HEADS), moba_k_gain),
                        _heads(v_m, MOBA_HEADS))
    return jnp.concatenate([o_nsa, o_moba], axis=-1) @ w_out

def sparse_moe(h, router_w, router_b, w1, b1, w2, b2):
    B, S, D = h.shape
    T = B * S
    hf = h.reshape(T, D)
    logits = (hf @ router_w + router_b).astype(jnp.float32)
    top_val, top_idx = lax.top_k(logits, TOP_K)
    gate = jax.nn.softmax(top_val, axis=-1)
    A = T * TOP_K
    e_flat = top_idx.reshape(A)
    tok_flat = jnp.arange(A, dtype=jnp.int32) // TOP_K
    w_flat = gate.reshape(A).astype(h.dtype)
    order = jnp.argsort(e_flat)
    e_s, tok_s, w_s = e_flat[order], tok_flat[order], w_flat[order]
    counts = jnp.bincount(e_flat, length=N_EXPERTS)
    padded = (counts + MOE_BLOCK - 1) // MOE_BLOCK * MOE_BLOCK
    start = jnp.cumsum(counts) - counts
    pend = jnp.cumsum(padded)
    pstart = pend - padded
    dest = pstart[e_s] + jnp.arange(A) - start[e_s]
    R = A + N_EXPERTS * MOE_BLOCK
    n_blocks = R // MOE_BLOCK
    row_tok = jnp.zeros((R,), jnp.int32).at[dest].set(tok_s)
    row_w = jnp.zeros((R,), h.dtype).at[dest].set(w_s)
    blk_e = jnp.minimum(jnp.searchsorted(pend, jnp.arange(n_blocks) * MOE_BLOCK, side='right'), N_EXPERTS - 1)

    def expert_block(args):
        e, toks, wts = args
        u = hf[toks] @ w1[e] + b1[e]
        g_, lin = u[:, :D_FF], u[:, D_FF:]
        g_ = jnp.minimum(g_, SWIGLU_LIMIT)
        lin = jnp.clip(lin, -SWIGLU_LIMIT, SWIGLU_LIMIT)
        y = ((lin + 1.0) * g_ * jax.nn.sigmoid(SWIGLU_ALPHA * g_)) @ w2[e] + b2[e]
        return y * wts[:, None]

    y = lax.map(expert_block, (blk_e, row_tok.reshape(n_blocks, MOE_BLOCK), row_w.reshape(n_blocks, MOE_BLOCK)))
    out = jax.ops.segment_sum(y.reshape(R, D), row_tok, num_segments=T)
    return out.reshape(B, S, D)

def first_inputs(seed: int = 0) -> dict:
    key = jax.random.key(seed)
    ks = jax.random.split(key, 21)
    n = jax.random.normal
    f32 = jnp.float32
    D = D_MODEL
    return {
        'x': n(ks[0], (BATCH, SEQ, D), f32),
        'c': n(ks[1], (BATCH, D), f32),
        'ada_w': n(ks[2], (DEPTH, D, 6 * D), f32) * (0.5 * D ** -0.5),
        'ada_b': n(ks[3], (DEPTH, 6 * D), f32) * 0.01,
        'ln1_g': 1.0 + 0.01 * n(ks[4], (DEPTH, D), f32),
        'ln2_g': 1.0 + 0.01 * n(ks[5], (DEPTH, D), f32),
        'w_in': n(ks[6], (DEPTH, D, IN_W), f32) * D ** -0.5,
        'nsa_q_gain': 1.0 + 0.01 * n(ks[7], (DEPTH, HEAD_DIM), f32),
        'nsa_k_gain': 1.0 + 0.01 * n(ks[8], (DEPTH, HEAD_DIM), f32),
        'nsa_cmp_pos': 0.1 * n(ks[9], (DEPTH, 2, NSA_CMP_LEN, HEAD_DIM), f32),
        'nsa_cmp_w1': n(ks[10], (DEPTH, 2, NSA_CMP_LEN * HEAD_DIM, NSA_CMP_HID), f32) * (NSA_CMP_LEN * HEAD_DIM) ** -0.5,
        'nsa_cmp_w2': n(ks[11], (DEPTH, 2, NSA_CMP_HID, HEAD_DIM), f32) * NSA_CMP_HID ** -0.5,
        'moba_q_gain': 1.0 + 0.01 * n(ks[12], (DEPTH, HEAD_DIM), f32),
        'moba_k_gain': 1.0 + 0.01 * n(ks[13], (DEPTH, HEAD_DIM), f32),
        'w_out': n(ks[14], (DEPTH, MIX_W, D), f32) * MIX_W ** -0.5,
        'router_w': n(ks[15], (DEPTH, D, N_EXPERTS), f32) * D ** -0.5,
        'router_b': 0.01 * n(ks[16], (DEPTH, N_EXPERTS), f32),
        'exp_w1': n(ks[17], (DEPTH, N_EXPERTS, D, 2 * D_FF), f32) * D ** -0.5,
        'exp_b1': 0.01 * n(ks[18], (DEPTH, N_EXPERTS, 2 * D_FF), f32),
        'exp_w2': n(ks[19], (DEPTH, N_EXPERTS, D_FF, D), f32) * D_FF ** -0.5,
        'exp_b2': 0.01 * n(ks[20], (DEPTH, N_EXPERTS, D), f32),
    }

def first_block(x, c, ada_w, ada_b, ln1_g, ln2_g, w_in, nsa_q_gain, nsa_k_gain, nsa_cmp_pos, nsa_cmp_w1,
              nsa_cmp_w2, moba_q_gain, moba_k_gain, w_out, router_w, router_b, exp_w1, exp_b1, exp_w2, exp_b2):
    cond = jax.nn.silu(c)
    for l in range(DEPTH):
        mod = (cond @ ada_w[l] + ada_b[l])[:, None, :]
        sh1, sc1, g1, sh2, sc2, g2 = jnp.split(mod, 6, axis=-1)
        h = rms_norm(x, ln1_g[l]) * (1.0 + sc1) + sh1
        x = x + g1 * hybrid_mixer(h, w_in[l], w_out[l], nsa_q_gain[l], nsa_k_gain[l], nsa_cmp_pos[l],
                                  nsa_cmp_w1[l], nsa_cmp_w2[l], moba_q_gain[l], moba_k_gain[l])
        h = rms_norm(x, ln2_g[l]) * (1.0 + sc2) + sh2
        x = x + g2 * sparse_moe(h, router_w[l], router_b[l], exp_w1[l], exp_b1[l], exp_w2[l], exp_b2[l])
    return x


DEPTH_2 = 2

N_META = 16
N_MIXERS = 2
SB_HEADS = 16
SB_HEAD_DIM = D_MODEL // SB_HEADS
Q_BLOCK = 128
LRU_WIDTH = D_MODEL
LRU_BLOCKS = 8
LRU_BLOCK_DIM = LRU_WIDTH // LRU_BLOCKS
CONV_WIDTH = 4
LRU_C = 8.0
D_FF_2 = 4 * D_MODEL
N_SB_LAYERS = (DEPTH_2 + 1) // 2
N_LRU_LAYERS = DEPTH_2 // 2


def rms_norm_2(x, g):
    xf = x.astype(jnp.float32)
    y = xf * lax.rsqrt(jnp.mean(xf * xf, axis=-1, keepdims=True) + EPS)
    return (y * g.astype(jnp.float32)).astype(x.dtype)

def _sb_block(q_blk, k, v, q_pos):
    t_len = k.shape[2]
    k_pos = jnp.arange(t_len)
    z = jnp.einsum('bhqd,bhkd->bhqk', q_blk, k).astype(jnp.float32) * (SB_HEAD_DIM ** -0.5)
    causal = k_pos[None, :] < q_pos[:, None]
    log_keep = jnp.where(causal, -jax.nn.softplus(z), 0.0)
    after = lax.cumsum(log_keep, axis=3, reverse=True) - log_keep
    w = jnp.where(causal, jnp.exp(jax.nn.log_sigmoid(z) + after), 0.0)
    return jnp.einsum('bhqk,bhkd->bhqd', w.astype(v.dtype), v)

def stick_breaking_mixer(x, w_qkv, w_o):
    b, t_len, _ = x.shape
    qkv = (x @ w_qkv).reshape(b, t_len, 3, SB_HEADS, SB_HEAD_DIM).transpose(2, 0, 3, 1, 4)
    q, k, v = qkv[0], qkv[1], qkv[2]
    meta_out = _sb_block(q[:, :, :N_META], k, v, jnp.arange(N_META))
    n_blk = (t_len - N_META) // Q_BLOCK
    q_real = q[:, :, N_META:].reshape(b, SB_HEADS, n_blk, Q_BLOCK, SB_HEAD_DIM).transpose(2, 0, 1, 3, 4)
    pos = N_META + jnp.arange(n_blk * Q_BLOCK).reshape(n_blk, Q_BLOCK)
    real_out = lax.map(lambda a: _sb_block(a[0], k, v, a[1]), (q_real, pos))
    real_out = real_out.transpose(1, 2, 0, 3, 4).reshape(b, SB_HEADS, n_blk * Q_BLOCK, SB_HEAD_DIM)
    o = jnp.concatenate([meta_out, real_out], axis=2)
    o = o.transpose(0, 2, 1, 3).reshape(b, t_len, D_MODEL)
    return o @ w_o

def _lru_combine(left, right):
    a1, b1 = left
    a2, b2 = right
    return a1 * a2, a2 * b1 + b2

def rglru_mixer(x, w_in, conv_w, conv_b, w_rg, b_rg, w_ig, b_ig, lam, w_out):
    b, t_len, _ = x.shape
    gate_in, rec_in = jnp.split(x @ w_in, 2, axis=-1)
    gate = jax.nn.gelu(gate_in)
    xp = jnp.pad(rec_in, ((0, 0), (CONV_WIDTH - 1, 0), (0, 0)))
    u = conv_b + sum(xp[:, j:j + t_len] * conv_w[j] for j in range(CONV_WIDTH))
    ub = u.reshape(b, t_len, LRU_BLOCKS, LRU_BLOCK_DIM)
    r = jax.nn.sigmoid(jnp.einsum('btni,nij->btnj', ub, w_rg).reshape(b, t_len, LRU_WIDTH) + b_rg)
    i = jax.nn.sigmoid(jnp.einsum('btni,nij->btnj', ub, w_ig).reshape(b, t_len, LRU_WIDTH) + b_ig)
    log_a = (-LRU_C * jax.nn.softplus(-lam.astype(jnp.float32))) * r.astype(jnp.float32)
    a = jnp.exp(log_a)
    mult = jnp.sqrt(-jnp.expm1(2.0 * log_a))
    bt = mult * (i * u).astype(jnp.float32)
    _, h = lax.associative_scan(_lru_combine, (a, bt), axis=1)
    y = h.astype(x.dtype) * gate
    return y @ w_out

def sq_relu_mlp(x, w_up, w_down):
    hdn = jax.nn.relu(x @ w_up)
    return (hdn * hdn) @ w_down

def second_inputs(seed: int = 0) -> dict:
    key = jax.random.key(seed)
    ks = jax.random.split(key, 20)
    f32 = jnp.float32
    D = D_MODEL

    def nrm(k, shape, scale):
        return jax.random.normal(k, shape, f32) * scale

    a0 = jax.random.uniform(ks[11], (N_LRU_LAYERS, LRU_WIDTH), f32, 0.9, 0.999)
    return {
        "x": nrm(ks[0], (BATCH, SEQ, D), 1.0),
        "meta_tokens": nrm(ks[1], (N_META, D), 1.0),
        "norm_mix": 1.0 + nrm(ks[2], (DEPTH_2, D), 0.02),
        "norm_mlp": 1.0 + nrm(ks[3], (DEPTH_2, D), 0.02),
        "sb_w_qkv": nrm(ks[4], (N_SB_LAYERS, D, 3 * D), D ** -0.5),
        "sb_w_o": nrm(ks[5], (N_SB_LAYERS, D, D), D ** -0.5),
        "lru_w_in": nrm(ks[6], (N_LRU_LAYERS, D, 2 * LRU_WIDTH), D ** -0.5),
        "lru_conv_w": nrm(ks[7], (N_LRU_LAYERS, CONV_WIDTH, LRU_WIDTH), CONV_WIDTH ** -0.5),
        "lru_conv_b": nrm(ks[8], (N_LRU_LAYERS, LRU_WIDTH), 0.01),
        "lru_w_rg": nrm(ks[9], (N_LRU_LAYERS, LRU_BLOCKS, LRU_BLOCK_DIM, LRU_BLOCK_DIM), LRU_BLOCK_DIM ** -0.5),
        "lru_b_rg": nrm(ks[10], (N_LRU_LAYERS, LRU_WIDTH), 0.01),
        "lru_w_ig": nrm(ks[12], (N_LRU_LAYERS, LRU_BLOCKS, LRU_BLOCK_DIM, LRU_BLOCK_DIM), LRU_BLOCK_DIM ** -0.5),
        "lru_b_ig": nrm(ks[13], (N_LRU_LAYERS, LRU_WIDTH), 0.01),
        "lru_lambda": jnp.log(a0) - jnp.log1p(-a0),
        "lru_w_out": nrm(ks[14], (N_LRU_LAYERS, LRU_WIDTH, D), LRU_WIDTH ** -0.5),
        "mlp_w_up": nrm(ks[15], (DEPTH_2, D, D_FF_2), D ** -0.5),
        "mlp_w_down": nrm(ks[16], (DEPTH_2, D_FF_2, D), D_FF_2 ** -0.5),
        "norm_final": 1.0 + nrm(ks[17], (D,), 0.02),
    }

def second_block(x, meta_tokens, norm_mix, norm_mlp, sb_w_qkv, sb_w_o, lru_w_in, lru_conv_w,
              lru_conv_b, lru_w_rg, lru_b_rg, lru_w_ig, lru_b_ig, lru_lambda, lru_w_out,
              mlp_w_up, mlp_w_down, norm_final):
    b = x.shape[0]
    meta = jnp.broadcast_to(meta_tokens[None].astype(x.dtype), (b, N_META, D_MODEL))
    h = jnp.concatenate([meta, x], axis=1)
    for i in range(DEPTH_2):
        hn = rms_norm_2(h, norm_mix[i])
        j = i // N_MIXERS
        if i % N_MIXERS == 0:
            h = h + stick_breaking_mixer(hn, sb_w_qkv[j], sb_w_o[j])
        else:
            h = h + rglru_mixer(hn, lru_w_in[j], lru_conv_w[j], lru_conv_b[j], lru_w_rg[j],
                                lru_b_rg[j], lru_w_ig[j], lru_b_ig[j], lru_lambda[j], lru_w_out[j])
        hn = rms_norm_2(h, norm_mlp[i])
        h = h + sq_relu_mlp(hn, mlp_w_up[i], mlp_w_down[i])
    h = rms_norm_2(h, norm_final)
    return h[:, N_META:]


def setup_inputs(seed=0):
    out = dict(first_inputs(seed))
    for name, value in second_inputs(seed + 1).items():
        if name != "x":
            out[name + "_2"] = value
    return out


def reference(
    x, c, ada_w, ada_b, ln1_g, ln2_g, w_in, nsa_q_gain, nsa_k_gain, nsa_cmp_pos, nsa_cmp_w1,
    nsa_cmp_w2, moba_q_gain, moba_k_gain, w_out, router_w, router_b, exp_w1, exp_b1, exp_w2,
    exp_b2, meta_tokens_2, norm_mix_2, norm_mlp_2, sb_w_qkv_2, sb_w_o_2, lru_w_in_2,
    lru_conv_w_2, lru_conv_b_2, lru_w_rg_2, lru_b_rg_2, lru_w_ig_2, lru_b_ig_2, lru_lambda_2,
    lru_w_out_2, mlp_w_up_2, mlp_w_down_2, norm_final_2,
):
    x = first_block(
        x, c, ada_w, ada_b, ln1_g, ln2_g, w_in, nsa_q_gain, nsa_k_gain, nsa_cmp_pos, nsa_cmp_w1,
        nsa_cmp_w2, moba_q_gain, moba_k_gain, w_out, router_w, router_b, exp_w1, exp_b1, exp_w2,
        exp_b2,
    )
    return second_block(
        x, meta_tokens_2, norm_mix_2, norm_mlp_2, sb_w_qkv_2, sb_w_o_2, lru_w_in_2,
        lru_conv_w_2, lru_conv_b_2, lru_w_rg_2, lru_b_rg_2, lru_w_ig_2, lru_b_ig_2,
        lru_lambda_2, lru_w_out_2, mlp_w_up_2, mlp_w_down_2, norm_final_2,
    )


_drawn_inputs = setup_inputs


def setup_inputs(seed=0):
    import zlib

    import numpy as np

    out = dict(_drawn_inputs(seed))
    spreads = {}
    factors = {'ada_b': 2.932,
     'ln1_g': 8.0,
     'ln2_g': 4.435,
     'nsa_q_gain': 8.0,
     'nsa_k_gain': 8.0,
     'nsa_cmp_pos': 3.545,
     'moba_q_gain': 8.0,
     'moba_k_gain': 8.0,
     'router_b': 3.46,
     'exp_b1': 8.0,
     'exp_b2': 42.502,
     'norm_mix_2': 3.074,
     'lru_conv_b_2': 49.584,
     'lru_b_rg_2': 200.0,
     'lru_b_ig_2': 163.539,
     'norm_final_2': 23.533,
     'norm_mlp_2': 6.531}
    for name, (base, spread) in spreads.items():
        noise = np.random.default_rng([zlib.crc32(name.encode()), seed]).standard_normal(out[name].shape)
        drawn = base * np.exp(spread * noise) if base else spread * noise
        out[name] = jnp.asarray(drawn.astype(out[name].dtype))
    for name, factor in factors.items():
        out[name] = (out[name] * factor).astype(out[name].dtype)
    return out
```

```python
from contextlib import ExitStack

import numpy as np

import concourse.bass as bass
from concourse import mybir

F32 = mybir.dt.float32
BF16 = mybir.dt.bfloat16
I32 = mybir.dt.int32
ALU = mybir.AluOpType
ACT = mybir.ActivationFunctionType
AX = mybir.AxisListType
ds = bass.ds

P = 128
D = 1024
C = D // P
T = 256
META = 16
TT = META + T
DH = 64
EXPERTS = 32
CAP = 64
CHUNKS = T // CAP
TOP_K = 4
FF = 1024
EPS = 1e-6
FAR = 1e33
NEG = -1e30
FLAT = 30.0
RING = 4
SLOT = 4096
ARENA = 28704

IN_CHUNKS = [(0, 512), (512, 512), (1024, 280), (1304, 512), (1816, 512), (2328, 512)]
IN_W = 2840
Z_KC, Z_VC, Z_KS, Z_VS, Z_KW, Z_VW, Z_G, Z_QM, Z_KM, Z_VM = 512, 640, 768, 896, 1024, 1152, 1280, 1304, 1816, 2328
HEAD_NORMS = {0: (0, 8, 0), 1: (Z_KS, 2, 8), 2: (Z_KW, 2, 10), 3: (Z_QM, 8, 12), 4: (Z_KM, 8, 20)}
HEAD_STATS = 28

A_LOADS = ([("ada", 0, k) for k in range(4)]
           + [load for c in range(6) for load in (("in", 0, c), ("ada", 1 + c // 4, c % 4))]
           + [("cmp", 0, 0), ("ada", 2, 2), ("ada", 2, 3)] + [("wout", 0, h) for h in range(2)])
A_CMP, A_N = A_LOADS.index(("cmp", 0, 0)), len(A_LOADS)
MOD_BANK = (6, 7, 6)
B_LOADS = ([("qkv", 0, c) for c in range(6)] + [("wo", 0, c) for c in range(2)]
           + [("up", 0, c) for c in range(8)] + [("down", 0, c) for c in range(8)]
           + [("lin", 0, c) for c in range(3)] + [("gates", 0, 0), ("lin", 0, 3)] + [("lout", 0, c) for c in range(2)]
           + [("up", 1, c) for c in range(8)] + [("down", 1, c) for c in range(8)])
B_QKV, B_WO, B_UP0, B_DOWN0, B_LIN, B_GATES, B_LIN3, B_LOUT, B_UP1, B_DOWN1 = 0, 6, 8, 16, 24, 27, 28, 29, 31, 39
DMAS_OF = {"wout": 4, "gates": 2}
PASS_LOADS = 6
MAX_PASSES = EXPERTS + T * TOP_K // CAP - 1

PC_C, PC_ADAB, PC_LN1, PC_LN2, PC_CONVW = 0, 8, 56, 64, 72
PC_CONVB, PC_BRG, PC_BIG, PC_LAM, PC_NMIX, PC_NMLP, PC_NFIN, PC_GAIN, PC_POS = 128, 136, 144, 152, 160, 176, 192, 200, 204
PARAM_ROWS = (104, 108)
PARAMS = ([("c", 0, 8), ("ada_b", 8, 48), ("ln1_g", 56, 8), ("ln2_g", 64, 8), ("lru_conv_w_2", 72, 32)],
          [("lru_conv_b_2", 0, 8), ("lru_b_rg_2", 8, 8), ("lru_b_ig_2", 16, 8), ("lru_lambda_2", 24, 8),
           ("norm_mix_2", 32, 16), ("norm_mlp_2", 48, 16), ("norm_final_2", 64, 8),
           ("nsa_cmp_pos", 76, 32)])
GAINS = ("nsa_q_gain", "nsa_k_gain", "moba_q_gain", "moba_k_gain")
M_SH1, M_SC1, M_G1, M_SH2, M_SC2, M_G2 = 0, 8, 16, 24, 32, 40

N_QKV, N_WO, N_UP0, N_DOWN0, N_LIN, N_GATE, N_LIN3, N_LOUT, N_UP1, N_DOWN1 = 0, 24, 32, 64, 72, 84, 100, 104, 112, 144

UNITS = 12
SCORES = 768


def slot_amounts(loads, first):
    amount, out = [0] * RING, []
    for n, (kind, *_) in enumerate(loads):
        r = (first + n) % RING
        amount[r] += 16 * DMAS_OF.get(kind, 1)
        out.append((r, amount[r]))
    return out, amount


A_AT, A_AMOUNT = slot_amounts(A_LOADS, 0)
B_AT, _ = slot_amounts(B_LOADS, A_N)


def a_freed(n):
    kind, layer, c = A_LOADS[n]
    return {"ada": ("mod_parts", 4 * layer + c + 1), "in": ("z_done", 2 * (c + 1)),
            "cmp": ("cmp_hidden", 1), "wout": ("wout_done", 4 * (c + 1))}[kind]


def pass_freed(p, part):
    return ("w1_parts", p * 4 + (part + 1)) if part < 4 else ("w2_parts", p * 2 + (part - 3))


def b_freed(n):
    kind, layer, c = B_LOADS[n]
    if kind == "down" and c % 4 < 3:
        return "down_parts", 6 * layer + 3 * (c // 4) + c % 4 + 1
    if kind == "down":
        return "chunk_done", (N_DOWN0, N_DOWN1)[layer] + 4 * (c // 4 + 1)
    if kind == "gates":
        return "chunk_done", N_GATE + 16
    if kind == "lin" and c == 3:
        return "chunk_done", N_LIN3 + 4
    first = {"qkv": N_QKV, "wo": N_WO, "lin": N_LIN, "lout": N_LOUT, "up": (N_UP0, N_UP1)[layer]}[kind]
    return "chunk_done", first + 4 * (c + 1)


def first_token(norm_number):
    return META if norm_number >= 3 else 0


def slope(head):
    return 2.0 ** -(head + 1)


class Chain:

    def __init__(self, eng, sem):
        self.eng, self.sem, self.n, self.base = eng, sem, 0, 0

    def link(self, ins):
        ins.then_inc(self.sem, 1)
        self.n += 1
        self.eng.wait_ge(self.sem, self.base + self.n)


class Area:

    def __init__(self, arena, at=0):
        self.arena, self.at = arena, at

    def take(self, *shape, dt=F32):
        size = int(np.prod(shape))
        words = size if dt in (F32, I32) else (size + 1) // 2
        part = self.arena[:, self.at:self.at + words]
        self.at += words
        assert self.at <= ARENA, self.at
        if dt != F32:
            part = part.bitcast(dt)
        names = "abcd"[:len(shape)]
        if len(shape) > 1:
            part = part.rearrange(f"p ({' '.join(names)}) -> p {' '.join(names)}",
                                  **{n: s for n, s in zip(names[1:], shape[1:])})
        return part


class Memory:

    def __init__(self, nc, ctx):
        def sb(name, shape, dt=F32):
            return ctx.enter_context(nc.sbuf_tensor(name, shape, dt))

        self.ring = sb("ring", [P, RING, SLOT])
        self.xT = sb("xT", [P, C, TT])
        self.hn = sb("hn", [P, C, TT])
        self.sq = sb("sq", [P, C, TT])
        self.rstd = sb("rstd", [P, TT])
        self.root = sb("root", [P, TT])
        self.prm = sb("prm", [P, 256])
        self.modT = sb("modT", [P, 48])
        self.ident = sb("ident", [P, P])
        self.ones = sb("ones", [P, P])
        self.eps = sb("eps", [P, 1])
        self.affine = sb("affine", [P, C])
        self.rw = sb("rw", [P, C, EXPERTS])
        self.rb = sb("rb", [1, EXPERTS])
        self.passes = sb("passes", [1, 1], I32)
        self.table = sb("table", [1, 2, 64], I32)
        self.lasts = sb("lasts", [1, EXPERTS], I32)
        self.ps = ctx.enter_context(nc.psum_tensor("ps", [P, 8, 512], F32))
        arena = sb("arena", [P, ARENA])

        a = Area(arena)
        self.x_tok = a.take(2, D)
        self.meta_tok = a.take(D)
        early_end = a.at
        self.params = a.take(2, P)
        self.cond = a.take(C)
        self.sig = a.take(C)
        self.condR = a.take(C, 32)
        self.modrow = a.take(512)
        self.gain8 = a.take(4)
        self.dist = a.take(384)
        self.cdist = a.take(2, 16)
        self.cmask = a.take(8, 2, 16)
        self.cbias = a.take(8, 2, 16)
        self.bias = a.take(4, SCORES)
        self.qT = a.take(2, 4, T)
        self.kA = a.take(2, 2, T)
        self.kM = a.take(4, 2, T)
        self.vcz = a.take(2, DH)
        self.cpz = a.take(8, P)
        self.probs0 = a.take(SCORES)
        self.PT = a.take(2, 2, 512)
        z_at = a.at
        self.z = a.take(2, IN_W)
        self.zsq = a.take(2, 512)
        self.ss = a.take(2, HEAD_STATS)
        self.hroot = a.take(2, HEAD_STATS)
        self.hrstd = a.take(2, HEAD_STATS)
        self.gates = a.take(2, 24)
        self.twice = a.take(2, 4, P)
        self.hid = a.take(P)
        self.hid2 = a.take(P)
        self.hidT = a.take(P)
        self.cw2 = a.take(2, DH)
        self.kcn = a.take(2, DH)
        self.kcz = a.take(2, 16)
        self.cstat = a.take(8)
        self.cs = a.take(16, 16)
        self.ce = a.take(16, 16)
        self.cmx = a.take(4, 16)
        self.fac = a.take(3, 8)
        self.sums = a.take(3, 4)
        self.nmax = a.take(3, 4)
        self.OT = a.take(C, T)
        self.blk = Area(arena).take(2, 16, CAP)
        a = Area(arena)
        self.scores = a.take(2, SCORES)
        self.probs12 = a.take(2, SCORES)
        assert a.at <= early_end

        a = Area(arena)
        self.h2 = a.take(2, D)
        self.acc = a.take(2, D)
        self.wtile = a.take(2, P)
        self.wT = a.take(2, P)
        self.b2 = a.take(D)
        self.b1 = a.take(2, FF)
        self.b1parts = a.take(2, FF, dt=BF16)
        self.he = a.take(512)
        self.hTe = a.take(4, P)
        self.g = a.take(512)
        self.lin = a.take(512)
        self.sg = a.take(512)
        self.act = a.take(512)
        self.aT = a.take(4, P)
        self.y = a.take(512)
        self.selz = a.take(2, T)
        assert a.at <= z_at
        a = Area(arena, z_at)
        self.padded = a.take(2, 36)
        self.marked = a.take(2, 36)
        self.top8 = a.take(2, 8)
        self.repl = a.take(2, 8)
        self.pick = a.take(2, EXPERTS)
        self.ew = a.take(2, EXPERTS)
        self.nbig = a.take(2)
        self.gsum = a.take(2)
        self.upper = a.take(P)
        self.key = a.take(2, CHUNKS * EXPERTS)
        self.wt = a.take(2, CHUNKS * EXPERTS)
        self.plan = a.take(6, EXPERTS)
        self.column = a.take(2)
        self.rowno = a.take(1)
        self.slots = a.take(P)
        self.sel = a.take(2, CAP)
        self.selw = a.take(2, P)
        self.eye3 = a.take(EXPERTS, dt=BF16)
        self.hot = a.take(CAP, dt=BF16)
        assert a.at <= ARENA - 2 * SLOT
        self.w2 = Area(arena, ARENA - 2 * SLOT).take(2, SLOT)

        a = Area(arena)
        self.bq = a.take(C, TT)
        self.bk = a.take(C, 2, TT)
        self.bv = a.take(C, TT)
        self.vtok = a.take(3, D)
        self.bO = a.take(C, TT)
        self.za = a.take(3, 2, 432)
        self.sp = a.take(2, 2, 432)
        self.w = a.take(2, 2, 432)
        self.lower = a.take(P)
        self.mones = a.take(P)
        self.bmask = a.take(432, dt=BF16)
        self.identb = a.take(P, dt=BF16)
        a = Area(arena)
        self.mlp = a.take(32, TT)
        self.relu = a.take(8, TT)
        a = Area(arena)
        self.gx = a.take(C, TT)
        self.g3 = a.take(C, TT)
        self.rec = a.take(C, TT + 4)
        self.u = a.take(C, TT)
        self.r = a.take(C, TT)
        self.ig = a.take(C, TT)
        self.la = a.take(C, TT)
        self.am = a.take(C, TT)
        self.th = a.take(C, TT)
        self.hs = a.take(C, TT)
        self.lamc = a.take(4, C)
        self.out_tok = Area(arena).take(2, D)

    def bank(self, b):
        return self.ps[:, b, :]


SEMAPHORES = """
x_loaded meta_loaded p0_loaded p1_loaded cw2_loaded router_loaded b1_loaded b2_loaded
ident_ready consts_ready pool_chain dve_chain act_chain dve_chain2
prm_turned prm_ready sig_ready cond_ready x_turned x_placed meta_placed squared norm_summed root_ready
mod_parts mod_rows mod_turned mod_ready h_ready
z_done z_copied doubled heads_ssq heads_root heads_normed gates_ready
turned turned_act turned_dve
cmp_hidden cmp_tanh_in cmp_tanh cmp_gelu cmp_hidT_done cmp_hidT cmp_kv_done cmp_kroot_in cmp_kroot
cmp_k_ready cmp_kT_done cmp_kT cmp_scored cmp_exp_in cmp_exp cmp_probs
scored biased maxed exped factored scaled flipped flipped_dve flipped_act o_parts o_copied
wout_done x1_ready x1_squared
logits_done top_ready gate_exp weights_ready ranks_done w_turned w_placed base_done h2_turned h2_placed
pool_moe routed split_ready
sel_ready gathered he_ready he_turned hTe_ready selt_done selz_ready selw_ready planned plan_turned w1_parts u_read g_ready sg_ready
a_ready a_turned aT_ready w2_parts y_ready scattered added
acc_turned x2_ready
b_root b_rstd b_squared b_h_ready
chunk_done down_parts chunk_dve chunk_act v_turned v_placed b_consts
b_scored b_clamped b_exp b_ln b_sp b_summed b_w b_o_done b_o_copied
mlp_ready
gate_tanh_in gate_tanh_in2 gate_tanh u_ready r_ready lam_in lam_out a_in a_exp mult_in mult_root lru_y
final_turned out_ready_dve out_ready_act out_stored
""".split()


class Signals:

    def __init__(self, nc, ctx):
        self.sem = {name: ctx.enter_context(nc.semaphore(name)) for name in SEMAPHORES}
        self.loaded = [ctx.enter_context(nc.semaphore(f"loaded{s}")) for s in range(RING)]
        self.w2_loaded = [ctx.enter_context(nc.semaphore(f"w2_loaded{s}")) for s in range(2)]
        self.b_loaded = [ctx.enter_context(nc.semaphore(f"b_loaded{s}")) for s in range(RING)]

    def __getitem__(self, name):
        return self.sem[name]


def program_sync(nc, sp, m, s, a):

    def slot(n):
        return m.ring[:, n, :]

    def source(kind, layer, c):
        if kind == "ada":
            src = a["ada_w"][0, 2 * P * c:2 * P * (c + 1), 2048 * layer:2048 * (layer + 1)]
            return [(slice(0, P), 4096, 2048, src.rearrange("(k p) n -> p k n", p=P))]
        if kind == "in":
            c0, w = IN_CHUNKS[c]
            return [(slice(0, P), 8 * w, w, a["w_in"][0, :, c0:c0 + w].rearrange("(k p) n -> p k n", p=P))]
        if kind == "cmp":
            return [(slice(0, P), 4096, P, a["nsa_cmp_w1"][0].rearrange("v (k p) n -> p (v k) n", p=P))]
        if kind == "wout":
            src = a["w_out"][0].rearrange("(b h i d) n -> b h d i n", b=2, h=2, i=4)
            return [(slice(64 * h, 64 * h + 64), 2048, 512, src[b, h, :, :, 512 * c:512 * c + 512])
                    for h in range(2) for b in range(2)]
        if kind == "gates":
            return [(slice(0, P), 1024, P, a[name][0].rearrange("n i j -> i n j"))
                    for name in ("lru_w_rg_2", "lru_w_ig_2")]
        if kind == "down":
            half, group = c // 4, c % 4
            src = a["mlp_w_down_2"][layer, D * group:D * (group + 1), 512 * half:512 * half + 512]
        else:
            name = {"qkv": "sb_w_qkv_2", "wo": "sb_w_o_2", "lin": "lru_w_in_2", "lout": "lru_w_out_2",
                    "up": "mlp_w_up_2"}[kind]
            if kind == "lin":
                c = (c + 2) % 4
            src = a[name][layer, :, 512 * c:512 * c + 512]
        return [(slice(0, P), 4096, 512, src.rearrange("(k p) n -> p k n", p=P))]

    def load(n, load_of, sem):
        for q, (rows, words, width, src) in enumerate(source(*load_of)):
            at = words * (q % 2)
            dst = m.ring[rows, n, at:at + words].rearrange("p (k n) -> p k n", n=width)
            sp.dma_start(dst, src).then_inc(sem, 16)

    def wait_for(signal):
        name, value = signal
        sp.wait_ge(s[name], value)

    sp.wait_ge(s["p0_loaded"], 16 * len(PARAMS[0]))
    for n, load_of in enumerate(A_LOADS):
        if n >= RING:
            wait_for(a_freed(n - RING))
        load(A_AT[n][0], load_of, s.loaded[A_AT[n][0]])

    def load_part(part, expert):
        if part < 4:
            r = (A_N + part) % RING
            src = a["exp_w1"][0, ds(expert, 1), 2 * P * part:2 * P * (part + 1), :]
            src = src.rearrange("e (k p) n -> p (e k) n", p=P)
            sp.dma_start(m.ring[:, r, :].rearrange("p (k n) -> p k n", n=2 * FF), src).then_inc(s.loaded[r], 16)
        else:
            src = a["exp_w2"][0, ds(expert, 1), 512 * (part - 4):512 * (part - 3), :]
            src = src.rearrange("e (k p) n -> p (e k) n", p=P)
            sp.dma_start(m.w2[:, part - 4, :].rearrange("p (k n) -> p k n", n=D),
                         src).then_inc(s.w2_loaded[part - 4], 16)

    for part in range(PASS_LOADS):
        if part < 4:
            wait_for(a_freed(A_N + part - RING))
        elif part == 4:
            sp.wait_ge(s["x1_ready"], C)
        load_part(part, 0)
    sp.wait_ge(s["routed"], 1)
    passes = sp.value_load(m.passes[0:1, 0:1], min_val=EXPERTS, max_val=MAX_PASSES)
    with sp.Fori(1, EXPERTS) as expert:
        last = sp.value_load(m.lasts[0:1, ds(expert - 1, 1)], min_val=0, max_val=MAX_PASSES - 1)
        for part in range(PASS_LOADS):
            wait_for(pass_freed(last, part))
            load_part(part, expert)

    sp.wait_ge(s["w1_parts"], passes * 4)
    for n, load_of in enumerate(B_LOADS):
        if n >= RING:
            wait_for(b_freed(n - RING))
        load(B_AT[n][0], load_of, s.b_loaded[B_AT[n][0]])


def program_gpsimd(nc, pool, m, s, a):
    g = nc.gpsimd
    chain = Chain(pool, s["pool_chain"])
    link = chain.link
    link(g.memset(m.ident[:], 0.0))
    link(g.affine_select(out=m.ident[:], in_=m.ident[:], pattern=[[-1, P]], compare_op=ALU.not_equal,
                         fill=1.0, base=0, channel_multiplier=1))
    link(g.memset(m.ones[:], 1.0))
    link(g.memset(m.eps[:], EPS))
    g.memset(m.kcz, 0.0).then_inc(s["ident_ready"], 1)
    g.memset(m.kA, 0.0).then_inc(s["consts_ready"], 1)
    g.memset(m.kM, 0.0).then_inc(s["consts_ready"], 1)
    g.memset(m.vcz, 0.0).then_inc(s["consts_ready"], 1)
    link(g.iota(m.dist[:, 0:P], pattern=[[-1, P]], base=0, channel_multiplier=1,
                allow_small_or_imprecise_dtypes=True))
    link(g.iota(m.dist[:, P:384], pattern=[[-1, 2 * P]], base=P, channel_multiplier=1,
                allow_small_or_imprecise_dtypes=True))
    link(g.affine_select(out=m.dist[:, 0:P], in_=m.dist[:, 0:P], pattern=[[-1, P]], compare_op=ALU.is_ge,
                         fill=FAR, base=0, channel_multiplier=1))
    link(g.affine_select(out=m.dist[:, P:384], in_=m.dist[:, P:384], pattern=[[-1, 2 * P]],
                         compare_op=ALU.is_ge, fill=FAR, base=P, channel_multiplier=1))
    link(g.iota(m.cdist, pattern=[[P, 2], [-16, 16]], base=-15, channel_multiplier=1,
                allow_small_or_imprecise_dtypes=True))
    link(g.tensor_scalar(m.cdist, m.cdist, -0.5, None, ALU.add))
    link(g.affine_select(out=m.cdist, in_=m.cdist, pattern=[[P, 2], [-16, 16]], compare_op=ALU.is_ge,
                         fill=FAR, base=-31, channel_multiplier=1))
    link(g.memset(m.cmask, 1.0))
    link(g.affine_select(out=m.cmask, in_=m.cmask, pattern=[[P, 2], [0, 8], [-16, 16]],
                         compare_op=ALU.is_ge, fill=0.0, base=-31, channel_multiplier=1))
    for i in range(4):
        for h in range(2):
            sl = slope(i + 4 * h)
            cb = m.cbias.rearrange("p (t i) h n -> p t i h n", t=2)[:, :, i, h, :]
            link(g.tensor_scalar(cb, m.cdist, -sl, None, ALU.mult))
            link(g.tensor_scalar(m.bias[:, i, 256 * h:256 * h + 256], m.dist[:, P:384], -sl, None, ALU.mult))
            link(g.tensor_scalar(m.bias[:, i, 512 + P * h:512 + P * h + P], m.dist[:, 0:P], -sl, None, ALU.mult))
    g.memset(m.cpz, 0.0).then_inc(s["consts_ready"], 1)

    pool.wait_ge(s["x_turned"], 5)
    g.memset(m.blk, 0.0).then_inc(s["doubled"], 1)
    pool.wait_ge(s["z_copied"], 4)
    for t in range(2):
        src = m.z[:, t, Z_KC:Z_KS].rearrange("p (g d) -> p g d", g=4).unsqueeze(2).to_broadcast([P, 4, 2, DH])
        g.tensor_copy(m.twice[:, t].rearrange("p g (c d) -> p g c d", c=2), src).then_inc(s["doubled"], 1)

    for u in range(UNITS):
        pool.wait_ge(s["factored"], u + 1)
        pr = probs_of(m, u)
        fac = m.fac[:, u % 3, :]
        for at, n, f in ((0, 256, 0), (512, P, 2)):
            v = pr[:, at:at + 2 * n].rearrange("p (h k) -> p h k", h=2)
            g.tensor_tensor(v, v, fac[:, f:f + 2].unsqueeze(2).to_broadcast([P, 2, n]),
                            ALU.mult).then_inc(s["scaled"], 1)

    pool.wait_ge(s["o_copied"], 8)
    g.memset(m.padded[:, :, EXPERTS:36], -3e38).then_inc(s["pool_moe"], 1)
    g.memset(m.repl, -3e38).then_inc(s["pool_moe"], 1)
    link(g.memset(m.upper, 1.0))
    link(g.affine_select(out=m.upper, in_=m.upper, pattern=[[1, P]], compare_op=ALU.is_gt, fill=0.0,
                         base=0, channel_multiplier=-1))
    link(g.iota(m.slots.rearrange("p (d n) -> p d n", d=2), pattern=[[0, 2], [1, CAP]], base=0,
                channel_multiplier=0, allow_small_or_imprecise_dtypes=True))
    link(g.iota(m.rowno, pattern=[[0, 1]], base=0, channel_multiplier=1,
                allow_small_or_imprecise_dtypes=True))
    link(g.memset(m.eye3, 1.0))
    link(g.memset(m.eye3[96:P, :], 0.0))
    for q in range(3):
        part = m.eye3[32 * q:32 * q + 32, :]
        link(g.affine_select(out=part, in_=part, pattern=[[-1, EXPERTS]], compare_op=ALU.is_equal,
                             fill=0.0, base=0, channel_multiplier=1))
    link(g.memset(m.key, -1.0))
    link(g.memset(m.wt, 0.0))
    link(g.memset(m.wtile, 0.0))
    link(g.memset(m.b2[EXPERTS:64, :], 0.0))
    link(g.memset(m.b2[64:P, :], 0.0))
    link(g.memset(m.y, 0.0))
    g.memset(m.selz, 0.0).then_inc(s["pool_moe"], 1)
    pool.wait_ge(s["pool_moe"], 3)
    link(g.memset(m.b1parts[96:P, :, :], 0.0))
    pool.wait_ge(s["b1_loaded"], 48)
    link(g.tensor_copy(m.b1parts[0:96, :, :], m.b1[0:96, :, :]))
    for q in (1, 2):
        for r in range(q, 3):
            rows = slice(32 * r, 32 * r + 32)
            link(g.tensor_tensor(m.b1[rows], m.b1[rows], m.b1parts[rows], ALU.subtract))
            link(g.tensor_copy(m.b1parts[rows], m.b1[rows]))
    g.memset(m.he[:, 0:1], 0.0).then_inc(s["split_ready"], 1)

    pool.wait_ge(s["x2_ready"], C)
    link(g.memset(m.lower, -1.0))
    link(g.affine_select(out=m.lower, in_=m.lower, pattern=[[-1, P]], compare_op=ALU.is_ge, fill=0.0,
                         base=0, channel_multiplier=1))
    link(g.memset(m.mones, -1.0))
    link(g.memset(m.identb, 0.0))
    link(g.affine_select(out=m.identb, in_=m.identb, pattern=[[-1, P]], compare_op=ALU.not_equal,
                         fill=1.0, base=0, channel_multiplier=1))
    link(g.memset(m.bmask, 0.0))
    for at, n in ((0, TT), (TT, TT - P), (2 * TT - P, META)):
        part = m.bmask[:, at:at + n]
        link(g.affine_select(out=part, in_=part, pattern=[[1, n]], compare_op=ALU.is_gt, fill=NEG,
                             base=0, channel_multiplier=-1))
    link(g.memset(m.bk, 0.0))
    link(g.memset(m.vtok[:, 2, :], 0.0))
    g.memset(m.za[:, 0, 0, 0:1], 0.0).then_inc(s["b_consts"], 1)

    pool.wait_ge(s["chunk_dve"], 52)
    x, x3 = m.gx[:, 0:4, :], m.g3[:, 0:4, :]
    link(g.tensor_tensor(x3, x, x, ALU.mult))
    link(g.tensor_scalar(x3, x3, GELU_A, 1.0, ALU.mult, ALU.add))
    g.tensor_tensor(x3, x3, x, ALU.mult).then_inc(s["gate_tanh_in"], 1)


def probs_of(m, u):
    return m.probs0 if u % 3 == 0 else m.probs12[:, u % 3 - 1, :]


def unit_of(u):
    return (0, u // 2, u % 2) if u < 8 else (1, u - 8, None)


def program_tensor(nc, pe, m, s, a):
    mm, turn = nc.tensor.matmul, nc.tensor.transpose
    ident = m.ident[:]
    bank = m.bank

    def a_slot(n):
        r, amount = A_AT[n]
        pe.wait_ge(s.loaded[r], amount)
        return m.ring[:, r, :]

    def b_slot(n):
        r, amount = B_AT[n]
        pe.wait_ge(s.b_loaded[r], amount)
        return m.ring[:, r, :].rearrange("p (k n) -> p k n", n=512)

    pe.wait_ge(s["ident_ready"], 1)
    def turn_params(out, n):
        rows = PARAM_ROWS[n]
        turn(out[:, 0:rows], m.params[0:rows, n, :], ident[0:rows, 0:rows]).then_inc(s["prm_turned"], 1)

    pe.wait_ge(s["p0_loaded"], 16 * len(PARAMS[0]))
    turn_params(bank(0), 0)
    pe.wait_ge(s["x_loaded"], 16)
    for b in range(4):
        for c in (2 * b, 2 * b + 1):
            for t in range(2):
                at = 256 * (c % 2) + P * t
                last = turn(bank(1 + b)[:, at:at + P], m.x_tok[:, t, P * c:P * c + P], ident)
        last.then_inc(s["x_turned"], 1)

    def sum_squares(signal, base, out, lo, per):
        for c in range(C):
            if c % per == 0:
                pe.wait_ge(s[signal], base + c // per + 1)
            last = mm(out, m.ones[:], m.sq[:, c, lo:TT], start=(c == 0), stop=(c == C - 1))
        last.then_inc(s["norm_summed"], 1)

    sum_squares("squared", 0, bank(7)[:, 0:T], META, 2)

    def modulation_part(group, k):
        w = a_slot(A_LOADS.index(("ada", group, k))).rearrange("p (k n) -> p k n", n=2048)
        for kk in range(2):
            for r in range(4):
                last = mm(bank(MOD_BANK[group])[32 * r:32 * r + 32, :], m.condR[:, 2 * k + kk, :],
                          w[:, kk, 512 * r:512 * r + 512], start=(k == 0 and kk == 0),
                          stop=(k == 3 and kk == 1))
        last.then_inc(s["mod_parts"], 1)

    def turn_modulation(group):
        pe.wait_ge(s["mod_rows"], group + 1)
        if group > 0:
            pe.wait_ge(s["mod_ready"], group)
        for q in range(4):
            last = turn(bank(5)[:, P * q:P * q + P], m.modrow[:, P * q:P * q + P], ident)
        last.then_inc(s["mod_turned"], 1)

    pe.wait_ge(s["cond_ready"], 1)
    for k in range(4):
        modulation_part(0, k)
    turn_modulation(0)
    pe.wait_ge(s["p1_loaded"], 16 * (len(PARAMS[1]) + 2 * len(GAINS)))
    pe.wait_ge(s["meta_loaded"], 16)
    pe.wait_ge(s["x_placed"], 4)
    turn_params(bank(4)[:, P:2 * P], 1)
    for c in range(C):
        last = turn(bank(4)[:, META * c:META * c + META], m.meta_tok[0:META, P * c:P * c + P],
                    ident[0:META, 0:META])
    last.then_inc(s["x_turned"], 1)

    for v in range(12):
        c, t = v // 2, v % 2
        w = IN_CHUNKS[c][1]
        if t == 0:
            wt = a_slot(A_LOADS.index(("in", 0, c)))[:, 0:8 * w].rearrange("p (k n) -> p k n", n=w)
        if v >= 4:
            pe.wait_ge(s["z_copied"], v - 3)
        elif v > 0:
            pe.wait_ge(s["x_placed"], v)
        for k in range(C):
            if v == 0:
                pe.wait_ge(s["h_ready"], k + 1)
            last = mm(bank(v % 4)[:, 0:w], m.hn[:, k, META + P * t:META + P * t + P], wt[:, k, :],
                      start=(k == 0), stop=(k == C - 1))
        last.then_inc(s["z_done"], 1)
        if t == 1:
            if v == 1:
                pe.wait_ge(s["root_ready"], 1)
            modulation_part(1 + c // 4, c % 4)

    def turned_pairs(b, at, i0):
        for i in (i0, i0 + 1):
            for t in range(2):
                col = 256 * (i - i0) + P * t
                last = turn(bank(b)[:, col:col + P], m.z[:, t, at + P * i:at + P * i + P], ident)
        last.then_inc(s["turned"], 1)

    def turned_twice(b, kv):
        for g in range(2):
            for t in range(2):
                col = 256 * g + P * t
                last = turn(bank(b)[:, col:col + P], m.twice[:, t, 2 * kv + g, :], ident)
        last.then_inc(s["turned"], 1)

    pe.wait_ge(s["consts_ready"], 4)
    pe.wait_ge(s["heads_normed"], 3)
    pe.wait_ge(s["z_copied"], 12)
    turned_pairs(0, 0, 0)
    turned_pairs(1, 0, 2)
    for n, at in enumerate((Z_KS, Z_KW)):
        for t in range(2):
            last = turn(bank(2)[:, 256 * n + P * t:256 * n + P * t + P], m.z[:, t, at:at + P], ident)
    last.then_inc(s["turned"], 1)
    pe.wait_ge(s["doubled"], 3)
    turned_twice(3, 0)
    pe.wait_ge(s["heads_normed"], 4)
    pe.wait_ge(s["turned_act"], 1)
    turned_pairs(0, Z_QM, 0)
    pe.wait_ge(s["turned_dve"], 1)
    turned_twice(1, 1)
    pe.wait_ge(s["turned_act"], 2)
    turned_pairs(2, Z_QM, 2)
    pe.wait_ge(s["heads_normed"], 5)
    pe.wait_ge(s["turned_dve"], 2)
    turned_pairs(3, Z_KM, 0)
    pe.wait_ge(s["turned_act"], 3)
    turned_pairs(0, Z_KM, 2)

    w = a_slot(A_CMP).rearrange("p (v k n) -> p v k n", v=2, k=16)
    pe.wait_ge(s["turned_dve"], 3)
    for k in range(16):
        for v in range(2):
            last = mm(bank(1)[64 * v:64 * v + 64, 0:P], m.blk[:, v, k, :], w[:, v, k, :],
                      start=(k == 0), stop=(k == 15))
    last.then_inc(s["cmp_hidden"], 1)
    modulation_part(2, 2)
    turn_modulation(1)
    pe.wait_ge(s["cmp_gelu"], 1)
    turn(bank(1)[:, 128:256], m.hid[:], ident).then_inc(s["cmp_hidT_done"], 1)
    pe.wait_ge(s["cmp_hidT"], 1)
    pe.wait_ge(s["cw2_loaded"], 16)
    for v in range(2):
        last = mm(bank(2)[0:64, 64 * v:64 * v + 64], m.hidT[:, 64 * v:64 * v + 64], m.cw2[:, v, :],
                  start=True, stop=True)
    last.then_inc(s["cmp_kv_done"], 1)
    modulation_part(2, 3)
    turn_modulation(2)
    pe.wait_ge(s["cmp_k_ready"], 1)
    turn(bank(2)[:, 256:320], m.kcn[0:64, :, :], ident[0:64, 0:64]).then_inc(s["cmp_kT_done"], 1)
    pe.wait_ge(s["cmp_kT"], 1)
    for t in range(2):
        for i in range(4):
            at = 32 * (4 * t + i)
            last = mm(bank(1)[:, at:at + 32], m.qT[:, 0, i, P * t:P * t + P], m.kcz, start=True, stop=True)
    last.then_inc(s["cmp_scored"], 1)

    def keys_of(u):
        q, i, branch = unit_of(u)
        return m.kA[:, :, branch, :] if q == 0 else m.kM[:, i, :, :]

    def score(u):
        q, i, _ = unit_of(u)
        b = 2 * (u % 2)
        keys = keys_of(u)
        mm(bank(b), m.qT[:, q, i, P:T], keys, start=True, stop=True)
        mm(bank(b + 1)[:, 0:2 * P], m.qT[:, q, i, 0:P], keys[:, :, 0:P],
           start=True, stop=True).then_inc(s["scored"], 1)

    def flip(u):
        q, i, branch = unit_of(u)
        pr = probs_of(m, u)
        for h in range(2):
            t1, t0 = pr[:, 256 * h:256 * h + 256], pr[:, 512 + P * h:512 + P * h + P]
            turn(bank(4 + h)[:, 0:P], t0, ident)
            turn(bank(4 + h)[:, P:2 * P], t1[:, 0:P], ident)
            last = turn(bank(4 + h)[:, 2 * P:3 * P], t1[:, P:2 * P], ident)
            if branch == 0:
                last = turn(bank(4 + h)[:, 3 * P:4 * P], m.cpz[:, 4 * h + i, :], ident)
            last.then_inc(s["flipped"], 1)

    def weigh(u):
        q, i, branch = unit_of(u)
        o = i if q == 0 else 4 + i
        out, pt = bank(6 + o % 2), m.PT[:, u % 2, :, :]
        rows = (slice(0, 64), slice(64, 128))
        if q == 0:
            vals = [(Z_VS, Z_VW)[branch] + DH * h for h in range(2)]
        else:
            vals = [Z_VM + DH * (i + 4 * h) for h in range(2)]
        if branch == 0:
            for h in range(2):
                mm(out[rows[h], 0:T], m.vcz[:, h, :], pt[:, :, 3 * P:4 * P], start=True, stop=False)
        for h in range(2):
            mm(out[rows[h], 0:T], m.z[:, 0, vals[h]:vals[h] + DH], pt[:, h, 0:T],
               start=(branch is None), stop=False)
        for h in range(2):
            last = mm(out[rows[h], P:T], m.z[:, 1, vals[h]:vals[h] + DH], pt[:, h, T:T + P],
                      start=False, stop=(branch != 0))
        last.then_inc(s["o_parts"], 1)

    pe.wait_ge(s["turned_act"], 5)
    pe.wait_ge(s["turned_dve"], 4)
    pe.wait_ge(s["mod_ready"], 3)
    for u in range(UNITS + 3):
        if u < UNITS:
            if u == 0:
                pe.wait_ge(s["cmp_exp_in"], 1)
            if u >= 2:
                pe.wait_ge(s["biased"], u - 1)
            score(u)
        if u >= 3:
            w_u = u - 3
            pe.wait_ge(s["flipped_dve"], w_u + 1)
            pe.wait_ge(s["flipped_act"], w_u + 1)
            q, i, branch = unit_of(w_u)
            o = i if q == 0 else 4 + i
            if o >= 2 and branch in (0, None):
                pe.wait_ge(s["o_copied"], o - 1)
            weigh(w_u)
        if 2 <= u < UNITS + 2:
            f = u - 2
            pe.wait_ge(s["scaled"], 2 * (f + 1))
            if f == 0:
                pe.wait_ge(s["cmp_probs"], 1)
            flip(f)

    pe.wait_ge(s["o_copied"], 8)
    for n in range(C):
        if n % 4 == 0:
            w = a_slot(A_LOADS.index(("wout", 0, n // 4))).rearrange("p (k n) -> p k n", n=512)
        if n >= 4:
            pe.wait_ge(s["x1_ready"], n - 3)
        for k in range(C):
            last = mm(bank(n % 4)[:, 0:T], w[:, k, P * (n % 4):P * (n % 4) + P], m.OT[:, k, :],
                      start=(k == 0), stop=(k == C - 1))
        last.then_inc(s["wout_done"], 1)
    sum_squares("x1_squared", 0, bank(7)[:, 0:T], META, 1)

    pe.wait_ge(s["router_loaded"], 32)
    for t in range(2):
        out = bank(4 + t)[:, 0:EXPERTS]
        mm(out, m.ones[0:1, :], m.rb[:], start=True, stop=False)
        for k in range(C):
            if t == 0:
                pe.wait_ge(s["h_ready"], C + k + 1)
            last = mm(out, m.hn[:, k, META + P * t:META + P * t + P], m.rw[:, k, :], start=False,
                      stop=(k == C - 1))
        last.then_inc(s["logits_done"], 1)
    for n in range(4):
        t, c0 = n // 2, 4 * (n % 2)
        for c in range(c0, c0 + 4):
            last = turn(bank(n)[:, P * (c - c0):P * (c - c0) + P],
                        m.hn[:, c, META + P * t:META + P * t + P], ident)
        last.then_inc(s["h2_turned"], 1)
    pe.wait_ge(s["pool_moe"], 3)
    pe.wait_ge(s["weights_ready"], 1)
    mm(bank(5)[:, 0:EXPERTS], m.upper, m.pick[:, 0, :], start=True, stop=True)
    mm(bank(5)[:, EXPERTS:2 * EXPERTS], m.ones[:], m.pick[:, 0, :], start=True, stop=False)
    mm(bank(5)[:, EXPERTS:2 * EXPERTS], m.upper, m.pick[:, 1, :], start=False, stop=True)
    mm(bank(5)[:, 2 * EXPERTS:3 * EXPERTS], m.ones[:], m.pick[:, 0, :], start=True, stop=False)
    mm(bank(5)[:, 2 * EXPERTS:3 * EXPERTS], m.ones[:], m.pick[:, 1, :], start=False,
       stop=True).then_inc(s["ranks_done"], 1)
    for t in range(2):
        last = turn(bank(4)[:, P + P * t:P + P * t + P], m.wtile[:, t, :], ident)
    last.then_inc(s["w_turned"], 1)
    pe.wait_ge(s["w_placed"], 1)
    pe.wait_ge(s["b2_loaded"], 16)
    pe.wait_ge(s["h2_placed"], 4)
    for n in range(4):
        t, h = n // 2, n % 2
        mm(bank(n), m.wT[:, t, :], m.b2[:, 512 * h:512 * h + 512], start=True,
           stop=True).then_inc(s["base_done"], 1)
    pe.wait_ge(s["planned"], 1)
    mm(bank(5)[0:1, P:2 * P], m.column[:, 0:1], ident, start=True, stop=True)
    mm(bank(5)[0:1, 2 * P:3 * P], m.column[:, 1:2], ident, start=True, stop=True).then_inc(s["plan_turned"], 1)

    def gather():
        for t in range(2):
            for h in range(2):
                last = mm(bank(0)[64 * h:64 * h + 64, :], m.sel[:, t, :],
                          m.h2[:, t, 512 * h:512 * h + 512], start=(t == 0), stop=(t == 1))
        last.then_inc(s["gathered"], 1)

    def turn_gathered():
        for j in range(4):
            last = turn(bank(1)[:, P * j:P * j + P], m.he[:, P * j:P * j + P], ident)
        last.then_inc(s["he_turned"], 1)

    def scatter(p):
        pe.wait_ge(s["y_ready"], p)
        pe.wait_ge(s["selz_ready"], p)
        for n in range(4):
            t, h = n // 2, n % 2
            pe.wait_ge(s["added"], p * 4 + (n + 3))
            mm(bank(6 + n % 2), m.selz[:, h, P * t:P * t + P], m.y, start=True,
               stop=True).then_inc(s["scattered"], 1)

    pe.wait_ge(s["added"], 4)
    pe.wait_ge(s["split_ready"], 1)
    pe.wait_ge(s["sel_ready"], 1)
    gather()
    pe.wait_ge(s["he_ready"], 1)
    turn_gathered()
    passes = pe.value_load(m.passes[0:1, 0:1], min_val=EXPERTS, max_val=MAX_PASSES)
    with pe.Fori(0, passes) as p:
        expert = pe.value_load(m.table[0:1, 1, ds(p, 1)], min_val=0, max_val=EXPERTS - 1)
        pe.wait_ge(s["hTe_ready"], p + 1)
        pe.wait_ge(s["u_read"], p)
        for part in range(2):
            for h in range(2):
                mm(bank(2 + part)[64 * h:64 * h + 64, :], m.hot,
                   m.b1parts[:, part, 512 * h:512 * h + 512], start=True, stop=False)
        for kk in range(4):
            r = (A_N + kk) % RING
            pe.wait_ge(s.loaded[r], expert * 16 + (A_AMOUNT[r] + 16))
            w = m.ring[:, r, :].rearrange("p (k n) -> p k n", n=2 * FF)
            for k in (2 * kk, 2 * kk + 1):
                lhs = m.hTe[:, k % 4, 64 * (k // 4):64 * (k // 4) + 64]
                for part in range(2):
                    for h in range(2):
                        at = FF * part + 512 * h
                        last = mm(bank(2 + part)[64 * h:64 * h + 64, :], lhs,
                                  w[:, k % 2, at:at + 512], start=False, stop=(k == C - 1))
            last.then_inc(s["w1_parts"], 1)
        pe.wait_ge(s["sel_ready"], p + 2)
        pe.wait_ge(s["selz_ready"], p)
        gather()
        scatter(p)
        pe.wait_ge(s["he_ready"], p + 2)
        turn_gathered()
        pe.wait_ge(s["selw_ready"], p + 1)
        for t in range(2):
            last = turn(bank(0)[:, P * t:P * t + P], m.selw[:, t, :], ident)
        last.then_inc(s["selt_done"], 1)
        pe.wait_ge(s["a_ready"], p + 1)
        for q in range(4):
            last = turn(bank(4)[:, P * q:P * q + P], m.act[:, P * q:P * q + P], ident)
        last.then_inc(s["a_turned"], 1)
        pe.wait_ge(s["aT_ready"], p + 1)
        for half in range(2):
            pe.wait_ge(s.w2_loaded[half], expert * 16 + 16)
            w = m.w2[:, half, :].rearrange("p (k n) -> p k n", n=D)
            for q in range(4):
                for h in range(2):
                    last = mm(bank(5)[64 * h:64 * h + 64, :], m.aT[:, q, 64 * half:64 * half + 64],
                              w[:, q, 512 * h:512 * h + 512], start=(half == 0 and q == 0),
                              stop=(half == 1 and q == 3))
            last.then_inc(s["w2_parts"], 1)
    scatter(passes)
    pe.wait_ge(s["added"], passes * 4 + 8)
    for n in range(C):
        for t in range(2):
            last = turn(bank(n)[:, P * t:P * t + P], m.acc[:, t, P * n:P * n + P], ident)
        last.then_inc(s["acc_turned"], 1)

    def dense(n0, load, act, lo=0, waits=None, made=None):
        w = b_slot(load)
        for q in range(4):
            if waits:
                waits(q)
            for k in range(C):
                if made and q == 0:
                    pe.wait_ge(s[made[0]], made[1] + k + 1)
                last = mm(bank((n0 + q) % 8)[:, lo:TT], w[:, k, P * q:P * q + P], act[:, k, lo:TT],
                          start=(k == 0), stop=(k == C - 1))
            last.then_inc(s["chunk_done"], 1)

    def norm(number):
        pe.wait_ge(s["b_squared"], C * (number + 1))
        lo = first_token(number)
        sum_squares("b_squared", C * number, bank(7)[:, lo:TT], lo, 1)

    pe.wait_ge(s["x2_ready"], C)
    norm(0)
    pe.wait_ge(s["b_rstd"], 1)
    for c in range(6):
        dense(N_QKV + 4 * c, B_QKV + c, m.hn, made=("b_h_ready", 0) if c == 0 else None,
              waits=(lambda q, c=c: pe.wait_ge(s["chunk_dve"], 4 * c + q - 7)) if c >= 2 else None)
    pe.wait_ge(s["b_consts"], 1)
    pe.wait_ge(s["chunk_dve"], 24)
    for n in range(6):
        t, h = n // 2, n % 2
        rows = min(P, TT - P * t)
        for q in range(4):
            last = turn(bank(n)[0:rows, P * q:P * q + P], m.bv[:, 4 * h + q, P * t:P * t + rows], ident)
        last.then_inc(s["v_turned"], 1)
    pe.wait_ge(s["v_placed"], 6)

    def b_score(i):
        for h in range(2):
            out = bank(2 * (i % 3) + h)
            mm(out[:, 0:432], m.identb, m.bmask, start=True, stop=False, skip_group_check=True)
            mm(out[:, 0:TT], m.bk[:, i, h, 0:P], m.bq[:, i, :], start=False, stop=False,
               skip_group_check=True)
            mm(out[:, TT:416], m.bk[:, i, h, P:2 * P], m.bq[:, i, P:TT], start=False, stop=False,
               skip_group_check=True)
            last = mm(out[0:META, 416:432], m.bk[:, i, h, 2 * P:TT], m.bq[:, i, 2 * P:TT],
                      start=False, stop=False, skip_group_check=True)
        last.then_inc(s["b_scored"], 1)

    def b_accumulate(i):
        for h in range(2):
            out, sp = bank(2 * (i % 3) + h), m.sp[:, i % 2, h, :]
            mm(out[:, 0:432], m.lower, sp, start=False, stop=False, skip_group_check=True)
            mm(out[:, P:TT], m.mones, sp[:, TT:416], start=False, stop=False, skip_group_check=True)
            mm(out[:, 256:TT], m.mones, sp[:, 416:432], start=False, stop=False, skip_group_check=True)
            last = mm(out[:, 400:416], m.mones, sp[:, 416:432], start=False, stop=True,
                      skip_group_check=True)
        last.then_inc(s["b_summed"], 1)

    def b_weigh(i):
        out = bank(6 + i % 2)
        for part, (q0, at) in enumerate(((0, 0), (P, TT), (2 * P, 416))):
            for h in range(2):
                v = m.vtok[:, part, P * i + DH * h:P * i + DH * h + DH]
                last = mm(out[64 * h:64 * h + 64, q0:TT], v, m.w[:, i % 2, h, at:at + TT - q0],
                          start=(part == 0), stop=(part == 2))
        last.then_inc(s["b_o_done"], 1)

    b_score(0)
    b_score(1)
    for i in range(9):
        if i < 8:
            pe.wait_ge(s["b_sp"], i + 1)
            b_accumulate(i)
        if i >= 1:
            pe.wait_ge(s["b_w"], i)
            if i >= 3:
                pe.wait_ge(s["b_o_copied"], i - 2)
            b_weigh(i - 1)
        if i + 2 < 8:
            b_score(i + 2)
    pe.wait_ge(s["b_o_copied"], 8)
    for c in range(2):
        dense(N_WO + 4 * c, B_WO + c, m.bO)

    def mlp(layer, n_up, n_down, l_up, l_down, norm_number, relu_before):
        lo = first_token(norm_number)
        norm(norm_number)
        for c in range(8):
            dense(n_up + 4 * c, l_up + c, m.hn, lo=lo, made=("b_h_ready", C * norm_number) if c == 0 else None,
                  waits=(lambda q, c=c: pe.wait_ge(s["chunk_act"], relu_before + 4 * c + q - 7))
                  if c >= 2 else None)
        pe.wait_ge(s["chunk_act"], relu_before + 32)
        for half in range(2):
            for group in range(4):
                w = b_slot(l_down + 4 * half + group)
                for q in range(4):
                    for k in range(C):
                        f = C * group + k
                        if half == 0 and q == 0:
                            pe.wait_ge(s["mlp_ready"], 32 * layer + f + 1)
                        last = mm(bank(4 * half + q)[:, lo:TT], w[:, k, P * q:P * q + P], m.mlp[:, f, lo:TT],
                                  start=(f == 0), stop=(f == 31))
                    if group == 3:
                        last.then_inc(s["chunk_done"], 1)
                if group < 3:
                    last.then_inc(s["down_parts"], 1)

    mlp(0, N_UP0, N_DOWN0, B_UP0, B_DOWN0, 1, 0)

    norm(2)
    for c in range(3):
        dense(N_LIN + 4 * c, B_LIN + c, m.hn, made=("b_h_ready", 2 * C) if c == 0 else None,
              waits=(lambda q: pe.wait_ge(s["chunk_dve"], 40 + q + 1)) if c == 2 else None)
    r, amount = B_AT[B_GATES]
    pe.wait_ge(s.b_loaded[r], amount)
    pe.wait_ge(s["u_ready"], C)
    pe.wait_ge(s["chunk_dve"], 52)
    gates = m.ring[:, r, 0:2048].rearrange("p (g n j) -> p g n j", g=2, n=8)
    for g in range(2):
        for n in range(8):
            if g == 1:
                pe.wait_ge(s["r_ready"], n + 1)
            mm(bank((N_GATE + n) % 8)[:, 0:TT], gates[:, g, n, :], m.u[:, n, :], start=True,
               stop=True).then_inc(s["chunk_done"], 1)
    dense(N_LIN3, B_LIN3, m.hn, waits=lambda q: pe.wait_ge(s["r_ready"], 8 + q + 1))
    pe.wait_ge(s["r_ready"], 16)
    pe.wait_ge(s["chunk_dve"], 56)
    for c in range(2):
        dense(N_LOUT + 4 * c, B_LOUT + c, m.hn, lo=META, made=("lru_y", 0) if c == 0 else None)

    mlp(1, N_UP1, N_DOWN1, B_UP1, B_DOWN1, 3, 32)

    norm(4)
    pe.wait_ge(s["b_h_ready"], 5 * C)
    for n in range(4):
        t, c0 = n // 2, 4 * (n % 2)
        for c in range(c0, c0 + 4):
            last = turn(bank(n)[:, P * (c - c0):P * (c - c0) + P],
                        m.hn[:, c, META + P * t:META + P * t + P], ident)
        last.then_inc(s["final_turned"], 1)


GELU_A, GELU_B = 0.044715, 0.7978845608028654


def program_scalar(nc, act, m, s, a):
    f = nc.scalar.activation
    bank = m.bank

    def copy(dst, src, name, scale=1.0):
        f(dst, src, ACT.Copy, scale=scale).then_inc(s[name], 1)

    for n in range(2):
        for q, (name, row, rows) in enumerate(PARAMS[n]):
            src = a[name]
            while len(src.shape) > 1:
                names = "abcd"[:len(src.shape)]
                src = src.rearrange(f"{' '.join(names)} -> ({' '.join(names)})")
            act.dma_start(m.params[row:row + rows, n, :],
                          src.rearrange("(r p) -> r p", p=P)).then_inc(s[f"p{n}_loaded"], 16)
            if n == 0 and q == 0:
                act.dma_start(m.x_tok, a["x"][0].rearrange("(t p) d -> p t d", p=P)).then_inc(s["x_loaded"], 16)
    for n, name in enumerate(GAINS):
        for h in range(2):
            row = PC_GAIN - P + n
            act.dma_start(m.params[row:row + 1, 1, DH * h:DH * h + DH], a[name]).then_inc(s["p1_loaded"], 16)
    act.dma_start(m.meta_tok[0:META, :], a["meta_tokens_2"]).then_inc(s["meta_loaded"], 16)
    act.dma_start(m.rw[:], a["router_w"][0].rearrange("(k p) e -> p k e", p=P)).then_inc(s["router_loaded"], 16)
    act.dma_start(m.rb[:], a["router_b"]).then_inc(s["router_loaded"], 16)
    act.dma_start(m.cw2, a["nsa_cmp_w2"][0].rearrange("v p d -> p v d")).then_inc(s["cw2_loaded"], 16)

    act.wait_ge(s["prm_ready"], 1)
    f(m.sig, m.prm[:, PC_C:PC_C + C], ACT.Sigmoid).then_inc(s["sig_ready"], 1)
    for b in range(4):
        act.wait_ge(s["x_turned"], b + 1)
        copy(m.xT[:, 2 * b:2 * b + 2, META:TT], bank(1 + b).rearrange("p (c t) -> p c t", c=2), "x_placed")
    for b in range(4):
        act.wait_ge(s["x_placed"], b + 1)
        xs = m.xT[:, 2 * b:2 * b + 2, META:TT]
        f(m.sq[:, 2 * b:2 * b + 2, META:TT], xs, ACT.Square).then_inc(s["squared"], 1)
    act.wait_ge(s["norm_summed"], 1)
    f(m.root[:, 0:T], bank(7)[:, 0:T], ACT.Sqrt, bias=m.eps[:], scale=1.0 / D).then_inc(s["root_ready"], 1)

    for v in range(12):
        c, t = v // 2, v % 2
        c0, w = IN_CHUNKS[c]
        act.wait_ge(s["z_done"], v + 1)
        dst, src = m.z[:, t, c0:c0 + w], bank(v % 4)[:, 0:w]
        if c in (0, 3, 4):
            dst = dst.rearrange("p (i h d) -> p i h d", h=2, i=4)
            src = src.rearrange("p (h i d) -> p i h d", h=2, i=4)
        copy(dst, src, "z_copied")
        if t == 1 and c in HEAD_NORMS:
            _, heads, s0 = HEAD_NORMS[c]
            act.wait_ge(s["heads_ssq"], c + 1)
            f(m.hroot[:, :, s0:s0 + heads], m.ss[:, :, s0:s0 + heads], ACT.Sqrt, bias=m.eps[:],
              scale=1.0 / DH).then_inc(s["heads_root"], 1)
    act.wait_ge(s["z_copied"], 6)
    f(m.gates, m.z[:, :, Z_G:Z_G + 24], ACT.Sigmoid).then_inc(s["gates_ready"], 1)

    def queries(n, b, q, i0, gain):
        act.wait_ge(s["turned"], n + 1)
        f(m.qT[:, q, i0:i0 + 2, :], bank(b).rearrange("p (i t) -> p i t", i=2), ACT.Copy,
          scale=gain).then_inc(s["turned_act"], 1)

    act.wait_ge(s["cond_ready"], 2)
    queries(0, 0, 0, 0, m.gain8[:, 0:1])
    act.wait_ge(s["turned"], 3)
    for h in range(2):
        rows = slice(64 * h, 64 * h + 64)
        last = f(m.kA[rows, h, :, :], bank(2)[rows, :].rearrange("p (b t) -> p b t", b=2), ACT.Copy,
                 scale=m.prm[rows, PC_GAIN + 1:PC_GAIN + 2])
    last.then_inc(s["turned_act"], 1)
    queries(4, 0, 1, 0, m.gain8[:, 2:3])
    queries(6, 2, 1, 2, m.gain8[:, 2:3])
    act.wait_ge(s["turned"], 9)
    for h in range(2):
        rows = slice(64 * h, 64 * h + 64)
        last = f(m.kM[rows, 2:4, h, :], bank(0)[rows, :].rearrange("p (i t) -> p i t", i=2), ACT.Copy,
                 scale=m.prm[rows, PC_GAIN + 3:PC_GAIN + 4])
    last.then_inc(s["turned_act"], 1)

    act.wait_ge(s["cmp_tanh_in"], 1)
    f(m.hid2, m.hid2, ACT.Tanh, scale=GELU_B).then_inc(s["cmp_tanh"], 1)
    act.wait_ge(s["cmp_kroot_in"], 1)
    f(m.cstat[0:64, 1:2], m.cstat[0:64, 0:1], ACT.Sqrt, bias=m.eps[0:64, :],
      scale=1.0 / DH).then_inc(s["cmp_kroot"], 1)
    act.wait_ge(s["cmp_exp_in"], 1)
    f(m.ce, m.cs, ACT.Exp).then_inc(s["cmp_exp"], 1)

    for u in range(UNITS + 4):
        if u < UNITS:
            act.wait_ge(s["maxed"], u + 1)
            if u >= 3:
                act.wait_ge(s["flipped"], 2 * (u - 2))
            sc, pr = m.scores[:, u % 2, :], probs_of(m, u)
            for q, (at, n) in enumerate(((0, 256), (256, 256), (512, P), (640, P))):
                last = f(pr[:, at:at + n], sc[:, at:at + n], ACT.Exp, bias=m.nmax[:, u % 3, q:q + 1],
                         accum_out=m.sums[:, u % 3, q:q + 1])
            last.then_inc(s["exped"], 1)
        if 2 <= u < UNITS + 2:
            n = u - 2
            width = 512 if unit_of(n)[2] == 0 else 384
            act.wait_ge(s["flipped"], 2 * n + 2)
            if n >= 2:
                act.wait_ge(s["o_parts"], n - 1)
            copy(m.PT[:, n % 2, 1, 0:width], bank(5)[:, 0:width], "flipped_act")
        if u >= 4:
            q, i, branch = unit_of(u - 4)
            if branch != 0:
                o = i if q == 0 else 4 + i
                act.wait_ge(s["o_parts"], u - 3)
                copy(m.OT[:, o, :], bank(6 + o % 2)[:, 0:T], "o_copied")
    act.wait_ge(s["o_copied"], 8)
    for q in range(3):
        act.dma_start(m.b1[32 * q:32 * q + 32, :, :],
                      a["exp_b1"][0].rearrange("e (g n) -> e g n", g=2)).then_inc(s["b1_loaded"], 16)
    act.wait_ge(s["pool_moe"], 3)
    act.dma_start(m.b2[0:EXPERTS, :], a["exp_b2"][0]).then_inc(s["b2_loaded"], 16)

    for c in range(C):
        act.wait_ge(s["x1_ready"], c + 1)
        f(m.sq[:, c, META:TT], m.xT[:, c, META:TT], ACT.Square).then_inc(s["x1_squared"], 1)
    act.wait_ge(s["norm_summed"], 2)
    f(m.root[:, 0:T], bank(7)[:, 0:T], ACT.Sqrt, bias=m.eps[:], scale=1.0 / D).then_inc(s["root_ready"], 1)
    for t in range(2):
        act.wait_ge(s["top_ready"], t + 1)
        f(m.ew[:, t, :], m.padded[:, t, 0:EXPERTS], ACT.Exp, bias=m.nbig[:, t:t + 1]).then_inc(s["gate_exp"], 1)
    for n in range(4):
        act.wait_ge(s["h2_turned"], n + 1)
        copy(m.h2[:, n // 2, 512 * (n % 2):512 * (n % 2) + 512], bank(n), "h2_placed")

    act.wait_ge(s["gathered"], 1)
    copy(m.he, bank(0), "he_ready")
    passes = act.value_load(m.passes[0:1, 0:1], min_val=EXPERTS, max_val=MAX_PASSES)
    nc.scalar.preload_act_table(ACT.Sigmoid)
    with act.Fori(0, passes) as p:
        act.wait_ge(s["g_ready"], p + 1)
        f(m.sg, m.g, ACT.Sigmoid, scale=1.702).then_inc(s["sg_ready"], 1)
        act.wait_ge(s["gathered"], p + 2)
        copy(m.he, bank(0), "he_ready")
        act.wait_ge(s["selt_done"], p + 1)
        f(m.selz[0:64, 0, :], bank(0)[0:64, 0:T], ACT.Copy)
        copy(m.selz[64:P, 1, :], bank(0)[64:P, 0:T], "selz_ready")
        act.wait_ge(s["a_turned"], p + 1)
        copy(m.aT, bank(4).rearrange("p (q n) -> p q n", q=4), "aT_ready")
        act.wait_ge(s["w2_parts"], p * 2 + 2)
        copy(m.y, bank(5), "y_ready")

    def norm(number, waits):
        lo = first_token(number)
        for c in range(C):
            act.wait_ge(s[waits[0]], waits[1] + c + 1)
            f(m.sq[:, c, lo:TT], m.xT[:, c, lo:TT], ACT.Square).then_inc(s["b_squared"], 1)
        act.wait_ge(s["norm_summed"], 3 + number)
        f(m.root[:, lo:TT], bank(7)[:, lo:TT], ACT.Sqrt, bias=m.eps[:], scale=1.0 / D).then_inc(s["b_root"], 1)

    norm(0, ("x2_ready", 0))

    def soft(i):
        act.wait_ge(s["b_clamped"], i + 1)
        f(m.za[:, i % 3], m.za[:, i % 3], ACT.Exp).then_inc(s["b_exp"], 1)
        act.wait_ge(s["b_exp"], i + 1)
        f(m.za[:, i % 3], m.za[:, i % 3], ACT.Ln, bias=m.ones[:, 0:1]).then_inc(s["b_ln"], 1)

    soft(0)
    soft(1)
    for i in range(8):
        act.wait_ge(s["b_summed"], i + 1)
        if i >= 2:
            act.wait_ge(s["b_o_done"], i - 1)
        q = 2 * (i % 3)
        f(m.w[:, i % 2], m.ps[:, q:q + 2, 0:432], ACT.Exp).then_inc(s["b_w"], 1)
        if i + 2 < 8:
            soft(i + 2)
    norm(1, ("chunk_dve", 24))

    def relus(layer, n_up):
        lo = first_token(1 + 2 * layer)
        for n in range(32):
            act.wait_ge(s["chunk_done"], n_up + n + 1)
            if 32 * layer + n >= 8:
                act.wait_ge(s["mlp_ready"], 32 * layer + n - 7)
            f(m.relu[:, n % 8, lo:TT], bank(n % 8)[:, lo:TT], ACT.Relu).then_inc(s["chunk_act"], 1)

    relus(0, N_UP0)
    norm(2, ("chunk_dve", 32))

    act.wait_ge(s["lam_in"], 1)
    f(m.lamc[:, 0, :], m.lamc[:, 0, :], ACT.Exp, scale=-1.0).then_inc(s["act_chain"], 1)
    act.wait_ge(s["act_chain"], 1)
    f(m.lamc[:, 0, :], m.lamc[:, 0, :], ACT.Ln, bias=m.ones[:, 0:1]).then_inc(s["lam_out"], 1)
    def gate_tanh(h):
        act.wait_ge(s[("gate_tanh_in", "gate_tanh_in2")[h]], 1)
        x3 = m.g3[:, 4 * h:4 * h + 4, :]
        f(x3, x3, ACT.Tanh, scale=GELU_B).then_inc(s["gate_tanh"], 1)

    for g in range(2):
        for n in range(C):
            act.wait_ge(s["chunk_done"], N_GATE + 8 * g + n + 1)
            f((m.r, m.ig)[g][:, n, :], bank((N_GATE + n) % 8)[:, 0:TT], ACT.Sigmoid,
              bias=m.prm[:, (PC_BRG, PC_BIG)[g] + n:(PC_BRG, PC_BIG)[g] + n + 1]).then_inc(s["r_ready"], 1)
    act.wait_ge(s["a_in"], C)
    f(m.am, m.la, ACT.Exp).then_inc(s["a_exp"], 1)
    f(m.th, m.la, ACT.Tanh).then_inc(s["a_exp"], 1)
    gate_tanh(0)
    act.wait_ge(s["mult_in"], 1)
    f(m.th, m.th, ACT.Sqrt, scale=-1.0).then_inc(s["mult_root"], 1)
    gate_tanh(1)
    norm(3, ("chunk_dve", 56))
    relus(1, N_UP1)
    norm(4, ("chunk_dve", 64))
    for n in (1, 3):
        act.wait_ge(s["final_turned"], n + 1)
        copy(m.out_tok[:, n // 2, 512:D], bank(n), "out_ready_act")


def program_vector(nc, dve, m, s, a):
    v = nc.vector
    bank = m.bank
    chain = Chain(dve, s["dve_chain"])
    link = chain.link

    def col(at, n=1):
        return m.prm[:, at:at + n]

    dve.wait_ge(s["prm_turned"], 1)
    v.tensor_copy(m.prm[:, 0:PARAM_ROWS[0]], bank(0)[:, 0:PARAM_ROWS[0]]).then_inc(s["prm_ready"], 1)
    dve.wait_ge(s["prm_ready"], 1)
    dve.wait_ge(s["sig_ready"], 1)
    link(v.tensor_tensor(m.cond, col(PC_C, C), m.sig, ALU.mult))
    v.tensor_copy(m.condR, m.cond.unsqueeze(2).to_broadcast([P, C, 32])).then_inc(s["cond_ready"], 1)

    def modulation(group):
        dve.wait_ge(s["mod_parts"], 4 * group + 4)
        if group > 0:
            dve.wait_ge(s["mod_turned"], group)
        v.tensor_copy(m.modrow, bank(MOD_BANK[group])).then_inc(s["mod_rows"], 1)
        dve.wait_ge(s["mod_turned"], group + 1)
        src = bank(5).rearrange("p (q r x) -> p r q x", q=4, r=4)[:, :, :, 0]
        dst = m.modT[:, 16 * group:16 * group + 16].rearrange("p (r q) -> p r q", r=4)
        bias = col(PC_ADAB + 16 * group, 16).rearrange("p (r q) -> p r q", r=4)
        v.tensor_tensor(dst, src, bias, ALU.add).then_inc(s["mod_ready"], 1)
        dve.wait_ge(s["mod_ready"], group + 1)

    def modulated_norm(number, gain, scale, shift):
        link(v.scalar_tensor_tensor(m.affine[:], m.modT[:, scale:scale + C], 1.0, col(gain, C), ALU.add, ALU.mult))
        dve.wait_ge(s["root_ready"], number)
        link(v.reciprocal(m.rstd[:, 0:T], m.root[:, 0:T]))
        first = chain.n
        for c in range(C):
            v.scalar_tensor_tensor(m.hn[:, c, META:TT], m.xT[:, c, META:TT], m.affine[:, c:c + 1],
                                   m.rstd[:, 0:T], ALU.mult, ALU.mult).then_inc(s["dve_chain"], 1)
        chain.n += C
        for c in range(C):
            dve.wait_ge(s["dve_chain"], first + c + 1)
            v.tensor_scalar(m.hn[:, c, META:TT], m.hn[:, c, META:TT], m.modT[:, shift + c:shift + c + 1],
                            None, ALU.add).then_inc(s["h_ready"], 1)

    modulation(0)
    dve.wait_ge(s["x_placed"], 4)
    modulated_norm(1, PC_LN1, M_SC1, M_SH1)
    dve.wait_ge(s["x_turned"], 5)
    v.tensor_copy(m.prm[:, P:P + PARAM_ROWS[1]], bank(4)[:, P:P + PARAM_ROWS[1]]).then_inc(s["prm_ready"], 1)
    v.tensor_copy(m.xT[:, :, 0:META], bank(4)[:, 0:P].rearrange("p (c t) -> p c t", c=C)).then_inc(s["meta_placed"], 1)
    dve.wait_ge(s["prm_ready"], 2)
    v.tensor_scalar(m.gain8, col(PC_GAIN, 4), DH ** -0.5, None, ALU.mult).then_inc(s["cond_ready"], 1)

    for c, (at, heads, s0) in HEAD_NORMS.items():
        w = DH * heads
        dve.wait_ge(s["z_copied"], 2 * c + 2)
        zs, ss, rs = m.z[:, :, at:at + w], m.ss[:, :, s0:s0 + heads], m.hrstd[:, :, s0:s0 + heads]
        link(v.tensor_tensor(m.zsq[:, :, 0:w], zs, zs, ALU.mult))
        v.tensor_reduce(ss, m.zsq[:, :, 0:w].rearrange("p t (h d) -> p t h d", d=DH), AX.X,
                        ALU.add).then_inc(s["heads_ssq"], 1)
        dve.wait_ge(s["heads_root"], c + 1)
        link(v.reciprocal(rs, m.hroot[:, :, s0:s0 + heads]))
        for t in range(2):
            zt = m.z[:, t, at:at + w].rearrange("p (h d) -> p h d", d=DH)
            last = v.tensor_tensor(zt, zt, m.hrstd[:, t, s0:s0 + heads].unsqueeze(2).to_broadcast([P, heads, DH]),
                                   ALU.mult)
        last.then_inc(s["heads_normed"], 1)

    dve.wait_ge(s["cond_ready"], 2)
    dve.wait_ge(s["turned"], 2)
    v.tensor_scalar(m.qT[:, 0, 2:4, :], bank(1).rearrange("p (i t) -> p i t", i=2), m.gain8[:, 0:1], None,
                    ALU.mult).then_inc(s["turned_dve"], 1)

    def blocks(kv, b, n):
        dve.wait_ge(s["turned"], n + 1)
        dve.wait_ge(s["doubled"], 1)
        for g in range(2):
            for l in range(2):
                rows = slice(64 * l, 64 * l + 64)
                src = bank(b)[rows, 256 * g:256 * g + 256].rearrange("p (n k l) -> p k n l", k=8, l=2)
                for k0 in range(2):
                    pos = m.prm[rows, PC_POS + 16 * kv + 8 * k0:PC_POS + 16 * kv + 8 * k0 + 8]
                    last = v.tensor_tensor(m.blk[rows, kv, 8 * k0:8 * k0 + 8, 32 * g:32 * g + 15],
                                           src[:, :, k0:k0 + 15, l],
                                           pos.unsqueeze(2).to_broadcast([64, 8, 15]), ALU.add)
        last.then_inc(s["turned_dve"], 1)

    blocks(0, 3, 3)
    blocks(1, 1, 5)
    dve.wait_ge(s["turned"], 8)
    for h in range(2):
        rows = slice(64 * h, 64 * h + 64)
        last = v.tensor_scalar(m.kM[rows, 0:2, h, :], bank(3)[rows, :].rearrange("p (i t) -> p i t", i=2),
                               m.prm[rows, PC_GAIN + 3:PC_GAIN + 4], None, ALU.mult)
    last.then_inc(s["turned_dve"], 1)

    dve.wait_ge(s["cmp_hidden"], 1)
    link(v.tensor_copy(m.hid, bank(1)[:, 0:P]))
    link(v.tensor_tensor(m.hid2, m.hid, m.hid, ALU.mult))
    link(v.tensor_scalar(m.hid2, m.hid2, GELU_A, 1.0, ALU.mult, ALU.add))
    v.tensor_tensor(m.hid2, m.hid2, m.hid, ALU.mult).then_inc(s["cmp_tanh_in"], 1)
    dve.wait_ge(s["cmp_tanh"], 1)
    link(v.scalar_tensor_tensor(m.hid2, m.hid2, 1.0, m.hid, ALU.add, ALU.mult))
    v.tensor_scalar(m.hid, m.hid2, 0.5, None, ALU.mult).then_inc(s["cmp_gelu"], 1)
    modulation(1)
    dve.wait_ge(s["cmp_hidT_done"], 1)
    v.tensor_copy(m.hidT, bank(1)[:, P:2 * P]).then_inc(s["cmp_hidT"], 1)
    dve.wait_ge(s["cmp_kv_done"], 1)
    link(v.tensor_copy(m.vcz[0:15, 0, :], bank(2)[0:15, 64:128]))
    link(v.tensor_copy(m.vcz[32:47, 1, :], bank(2)[32:47, 64:128]))
    link(v.tensor_copy(m.kcn[0:64, 0, :], bank(2)[0:64, 0:64]))
    link(v.tensor_tensor(m.hid2[0:64, 0:64], m.kcn[0:64, 0, :], m.kcn[0:64, 0, :], ALU.mult))
    v.tensor_reduce(m.cstat[0:64, 0:1], m.hid2[0:64, 0:64], AX.X, ALU.add).then_inc(s["cmp_kroot_in"], 1)
    dve.wait_ge(s["cmp_kroot"], 1)
    link(v.reciprocal(m.cstat[0:64, 2:3], m.cstat[0:64, 1:2]))
    link(v.tensor_scalar(m.kcn[0:64, 1, :], m.kcn[0:64, 0, :], m.cstat[0:64, 2:3], None, ALU.mult))
    v.tensor_copy(m.kcn[0:64, 0, :], m.kcn[0:64, 1, :]).then_inc(s["cmp_k_ready"], 1)
    modulation(2)
    dve.wait_ge(s["cmp_kT_done"], 1)
    for h in range(2):
        rows = slice(64 * h, 64 * h + 64)
        last = v.tensor_scalar(m.kcz[rows, h, 0:15], bank(2)[rows, 256 + 32 * h:256 + 32 * h + 15],
                               m.prm[rows, PC_GAIN + 1:PC_GAIN + 2], None, ALU.mult)
    last.then_inc(s["cmp_kT"], 1)
    dve.wait_ge(s["cmp_scored"], 1)
    link(v.tensor_tensor(m.cs, bank(1)[:, 0:256].rearrange("p (a n) -> p a n", a=16),
                         m.cbias.rearrange("p a h n -> p (a h) n"), ALU.add))
    link(v.tensor_reduce(m.cmx[:, 0, :], m.cs, AX.X, ALU.max))
    v.tensor_tensor(m.cs, m.cs, m.cmx[:, 0, :].unsqueeze(2).to_broadcast([P, 16, 16]),
                    ALU.subtract).then_inc(s["cmp_exp_in"], 1)
    dve.wait_ge(s["cmp_exp"], 1)
    link(v.tensor_reduce(m.cmx[:, 1, :], m.ce, AX.X, ALU.add))
    link(v.reciprocal(m.cmx[:, 2, :], m.cmx[:, 1, :]))
    dve.wait_ge(s["gates_ready"], 1)
    gate = m.gates.rearrange("p t (h i j) -> p t i h j", h=2, i=4)
    link(v.tensor_tensor(m.cmx[:, 3, :].rearrange("p (t i h) -> p t i h", t=2, i=4),
                         m.cmx[:, 2, :].rearrange("p (t i h) -> p t i h", t=2, i=4), gate[:, :, :, :, 0], ALU.mult))
    link(v.tensor_tensor(m.ce, m.ce, m.cmask.rearrange("p a h n -> p (a h) n"), ALU.mult))
    v.tensor_tensor(m.cpz.rearrange("p a (x n) -> p a x n", n=32)[:, :, 0:2, 0:15],
                    m.ce.rearrange("p (a h) n -> p a h n", h=2)[:, :, :, 0:15],
                    m.cmx[:, 3, :].rearrange("p (a h) -> p a h", h=2).unsqueeze(3).to_broadcast([P, 8, 2, 15]),
                    ALU.mult).then_inc(s["cmp_probs"], 1)

    for u in range(UNITS + 2):
        if u < UNITS:
            _, i, _ = unit_of(u)
            b = 2 * (u % 2)
            dve.wait_ge(s["scored"], u + 1)
            if u >= 2:
                dve.wait_ge(s["exped"], u - 1)
            sc = m.scores[:, u % 2, :]
            v.tensor_tensor(sc, m.ps[:, b:b + 2, :].rearrange("p b n -> p (b n)")[:, 0:SCORES],
                            m.bias[:, i, :], ALU.add).then_inc(s["biased"], 1)
            dve.wait_ge(s["biased"], u + 1)
            v.tensor_reduce(m.nmax[:, u % 3, 0:2], sc[:, 0:512].rearrange("p (h k) -> p h k", h=2), AX.X,
                            ALU.max, negate=True)
            v.tensor_reduce(m.nmax[:, u % 3, 2:4], sc[:, 512:768].rearrange("p (h k) -> p h k", h=2), AX.X,
                            ALU.max, negate=True).then_inc(s["maxed"], 1)
        if 1 <= u <= UNITS:
            n = u - 1
            q, i, branch = unit_of(n)
            dve.wait_ge(s["exped"], n + 1)
            sums, fac = m.sums[:, n % 3, :], m.fac[:, n % 3, :]
            if q == 0:
                link(v.reciprocal(fac[:, 4:8], sums))
                for t in (1, 0):
                    at = 2 * (1 - t)
                    last = v.tensor_tensor(fac[:, at:at + 2], fac[:, 4 + at:6 + at],
                                           gate[:, t, i, :, 1 + branch], ALU.mult)
            else:
                last = v.reciprocal(fac[:, 0:4], sums)
            last.then_inc(s["factored"], 1)
        if u >= 2:
            n = u - 2
            width = 512 if unit_of(n)[2] == 0 else 384
            dve.wait_ge(s["flipped"], 2 * n + 1)
            if n >= 2:
                dve.wait_ge(s["o_parts"], n - 1)
            v.tensor_copy(m.PT[:, n % 2, 0, 0:width], bank(4)[:, 0:width]).then_inc(s["flipped_dve"], 1)

    for n in range(C):
        dve.wait_ge(s["wout_done"], n + 1)
        xs = m.xT[:, n, META:TT]
        v.scalar_tensor_tensor(xs, bank(n % 4)[:, 0:T], m.modT[:, M_G1 + n:M_G1 + n + 1], xs, ALU.mult,
                               ALU.add).then_inc(s["x1_ready"], 1)
    dve.wait_ge(s["x1_ready"], C)
    modulated_norm(2, PC_LN2, M_SC2, M_SH2)

    dve.wait_ge(s["pool_moe"], 3)
    for t in range(2):
        dve.wait_ge(s["logits_done"], t + 1)
        link(v.tensor_copy(m.padded[:, t, 0:EXPERTS], bank(4 + t)[:, 0:EXPERTS]))
        link(v.max(m.top8[:, t, :], m.padded[:, t, 0:EXPERTS]))
        link(v.tensor_copy(m.repl[:, t, 0:TOP_K], m.top8[:, t, 0:TOP_K]))
        v.tensor_scalar(m.nbig[:, t:t + 1], m.top8[:, t, 0:1], -1.0, None, ALU.mult).then_inc(s["top_ready"], 1)
        link(v.match_replace(m.marked[:, t, :], m.repl[:, t, :], m.padded[:, t, :], 3e38))
        link(v.tensor_scalar(m.pick[:, t, :], m.marked[:, t, 0:EXPERTS], 3e38, None, ALU.is_equal))
        dve.wait_ge(s["gate_exp"], t + 1)
        link(v.tensor_tensor(m.ew[:, t, :], m.ew[:, t, :], m.pick[:, t, :], ALU.mult))
        link(v.tensor_reduce(m.gsum[:, t:t + 1], m.ew[:, t, :], AX.X, ALU.add))
        link(v.reciprocal(m.gsum[:, t:t + 1], m.gsum[:, t:t + 1]))
        last = v.tensor_scalar(m.wtile[:, t, 0:EXPERTS], m.ew[:, t, :], m.gsum[:, t:t + 1], None, ALU.mult)
        if t == 0:
            link(last)
    last.then_inc(s["weights_ready"], 1)
    dve.wait_ge(s["weights_ready"], 1)
    dve.wait_ge(s["ranks_done"], 1)
    for t in range(2):
        key = m.key[:, t, :]
        link(v.scalar_tensor_tensor(key[:, 0:EXPERTS], bank(5)[:, EXPERTS * t:EXPERTS * t + EXPERTS], 1.0,
                                    m.pick[:, t, :], ALU.add, ALU.mult))
        link(v.tensor_scalar(key[:, 0:EXPERTS], key[:, 0:EXPERTS], -1.0, None, ALU.add))
        for c in range(1, CHUNKS):
            link(v.tensor_scalar(key[:, EXPERTS * c:EXPERTS * (c + 1)], key[:, 0:EXPERTS], -float(CAP * c),
                                 None, ALU.add))
        link(v.tensor_copy(m.wt[:, t, 0:CHUNKS * EXPERTS].rearrange("p (c e) -> p c e", c=CHUNKS),
                           m.wtile[:, t, 0:EXPERTS].unsqueeze(1).to_broadcast([P, CHUNKS, EXPERTS])))
    dve.wait_ge(s["w_turned"], 1)
    v.tensor_copy(m.wT, bank(4)[:, P:3 * P].rearrange("p (t n) -> p t n", t=2)).then_inc(s["w_placed"], 1)
    needed, upto, first, behind, inside, code = (m.plan[:, q, :] for q in range(6))
    count = bank(5)[:, 2 * EXPERTS:3 * EXPERTS]
    link(v.tensor_scalar(needed, count, float(CAP), 1.0, ALU.is_gt, ALU.add))
    for c in range(2, CHUNKS):
        link(v.scalar_tensor_tensor(needed, count, float(CAP * c), needed, ALU.is_gt, ALU.add))
    link(v.tensor_tensor_scan(upto, m.ones[:, 0:EXPERTS], needed, 0.0, ALU.mult, ALU.add))
    link(v.tensor_copy(m.passes[:], upto[0:1, EXPERTS - 1:EXPERTS]))
    link(v.tensor_scalar(m.lasts[:], upto[0:1, :], -1.0, None, ALU.add))
    link(v.tensor_tensor(first, upto, needed, ALU.subtract))
    link(v.tensor_scalar(behind, first, -1.0, m.rowno, ALU.mult, ALU.add))
    link(v.tensor_tensor(inside, needed, behind, ALU.is_gt))
    link(v.scalar_tensor_tensor(inside, behind, 0.0, inside, ALU.is_ge, ALU.mult))
    link(v.scalar_tensor_tensor(code, behind, float(EXPERTS), m.slots[:, 0:EXPERTS], ALU.mult, ALU.add))
    link(v.tensor_tensor(code, code, inside, ALU.mult))
    link(v.tensor_reduce(m.column[:, 0:1], code, AX.X, ALU.add))
    link(v.tensor_tensor(code, m.slots[:, 0:EXPERTS], inside, ALU.mult))
    v.tensor_reduce(m.column[:, 1:2], code, AX.X, ALU.add).then_inc(s["planned"], 1)
    dve.wait_ge(s["plan_turned"], 1)
    v.tensor_copy(m.table[:], bank(5)[0:1, P:3 * P].rearrange("p (a n) -> p a n", a=2)[:, :, 0:64]).then_inc(
        s["routed"], 1)
    for n in range(4):
        dve.wait_ge(s["base_done"], n + 1)
        v.tensor_copy(m.acc[:, n // 2, 512 * (n % 2):512 * (n % 2) + 512], bank(n)).then_inc(s["added"], 1)

    def code_of(p):
        return dve.value_load(m.table[0:1, 0, ds(p, 1)], min_val=0, max_val=CHUNKS * EXPERTS - 1)

    def select(code):
        for t in range(2):
            v.tensor_scalar(m.sel[:, t, :], m.slots[:, 0:CAP], m.key[:, t, ds(code, 1)], None, ALU.is_equal)
        v.tensor_copy(m.hot, m.eye3[:, ds(code & (EXPERTS - 1), 1)].to_broadcast([P, CAP])).then_inc(
            s["sel_ready"], 1)

    def turned_gather():
        v.tensor_copy(m.hTe, bank(1).rearrange("p (j n) -> p j n", j=4)).then_inc(s["hTe_ready"], 1)

    def add(p):
        for n in range(4):
            t, h = n // 2, n % 2
            dve.wait_ge(s["scattered"], p * 4 + (n + 1))
            dve.wait_ge(s["added"], p * 4 + (n + 1))
            part = m.acc[:, t, 512 * h:512 * h + 512]
            v.tensor_tensor(part, bank(6 + n % 2), part, ALU.add).then_inc(s["added"], 1)

    dve.wait_ge(s["routed"], 1)
    select(code_of(0))
    dve.wait_ge(s["he_turned"], 1)
    turned_gather()
    passes = dve.value_load(m.passes[0:1, 0:1], min_val=EXPERTS, max_val=MAX_PASSES)
    with dve.Fori(0, passes) as p:
        code, next_code = code_of(p), code_of(p + 1)
        dve.wait_ge(s["w1_parts"], p * 4 + 1)
        select(next_code)
        v.tensor_scalar(m.selw[:, 0, :], m.slots, m.key[:, 0, ds(code, 1)], m.wt[:, 0, ds(code, 1)],
                        ALU.is_equal, ALU.mult)
        v.tensor_scalar(m.selw[:, 1, :], m.slots, m.key[:, 1, ds(code, 1)], m.wt[:, 1, ds(code, 1)],
                        ALU.is_equal, ALU.mult).then_inc(s["selw_ready"], 1)
        dve.wait_ge(s["w1_parts"], p * 4 + 4)
        v.tensor_scalar(m.g, bank(2), 7.0, None, ALU.min).then_inc(s["g_ready"], 1)
        v.tensor_scalar(m.lin, bank(3), 7.0, -7.0, ALU.min, ALU.max).then_inc(s["u_read"], 1)
        dve.wait_ge(s["u_read"], p + 1)
        v.scalar_tensor_tensor(m.act, m.lin, 1.0, m.g, ALU.add, ALU.mult).then_inc(s["dve_chain2"], 1)
        dve.wait_ge(s["dve_chain2"], p + 1)
        dve.wait_ge(s["sg_ready"], p + 1)
        v.tensor_tensor(m.act, m.act, m.sg, ALU.mult).then_inc(s["a_ready"], 1)
        add(p)
        dve.wait_ge(s["he_turned"], p + 2)
        turned_gather()
    add(passes)
    for n in range(C):
        dve.wait_ge(s["acc_turned"], n + 1)
        xs = m.xT[:, n, META:TT]
        v.scalar_tensor_tensor(xs, bank(n)[:, 0:T], m.modT[:, M_G2 + n:M_G2 + n + 1], xs, ALU.mult,
                               ALU.add).then_inc(s["x2_ready"], 1)

    def norm(number, gain):
        dve.wait_ge(s["b_root"], number + 1)
        lo = first_token(number)
        v.reciprocal(m.rstd[:, lo:TT], m.root[:, lo:TT]).then_inc(s["b_rstd"], 1)
        dve.wait_ge(s["b_rstd"], number + 1)
        for c in range(C):
            v.scalar_tensor_tensor(m.hn[:, c, lo:TT], m.xT[:, c, lo:TT], col(gain + c), m.rstd[:, lo:TT], ALU.mult,
                                   ALU.mult).then_inc(s["b_h_ready"], 1)

    def residual(n0, done, lo=0):
        for n in range(C):
            dve.wait_ge(s["chunk_done"], n0 + n + 1)
            v.tensor_tensor(m.xT[:, n, lo:TT], bank(n)[:, lo:TT], m.xT[:, n, lo:TT], ALU.add).then_inc(s["chunk_dve"], 1)
        dve.wait_ge(s["chunk_dve"], done + C)

    norm(0, PC_NMIX)
    for n in range(24):
        dve.wait_ge(s["chunk_done"], n + 1)
        src = bank(n % 8)[:, 0:TT]
        if n == 8:
            dve.wait_ge(s["b_consts"], 1)
        if n < 8:
            last = v.tensor_scalar(m.bq[:, n, :], src, DH ** -0.5, None, ALU.mult)
        elif n < 16:
            for h in range(2):
                rows = slice(64 * h, 64 * h + 64)
                last = v.tensor_copy(m.bk[rows, n - 8, h, :], src[rows, :])
        else:
            last = v.tensor_copy(m.bv[:, n - 16, :], src)
        last.then_inc(s["chunk_dve"], 1)
    for n in range(6):
        t, h = n // 2, n % 2
        rows = min(P, TT - P * t)
        dve.wait_ge(s["v_turned"], n + 1)
        v.tensor_copy(m.vtok[0:rows, t, 512 * h:512 * h + 512], bank(n)[0:rows, :]).then_inc(s["v_placed"], 1)

    def clamped(i):
        q = 2 * (i % 3)
        dve.wait_ge(s["b_scored"], i + 1)
        if i >= 3:
            dve.wait_ge(s["b_sp"], i - 2)
        v.tensor_scalar(m.za[:, i % 3], m.ps[:, q:q + 2, 0:432], FLAT, None, ALU.min).then_inc(s["b_clamped"], 1)

    def head_output(i):
        dve.wait_ge(s["b_o_done"], i + 1)
        v.tensor_copy(m.bO[:, i, :], bank(6 + i % 2)[:, 0:TT]).then_inc(s["b_o_copied"], 1)

    def softplus(i):
        q = 2 * (i % 3)
        dve.wait_ge(s["b_ln"], i + 1)
        if i >= 2:
            dve.wait_ge(s["b_summed"], i - 1)
        v.tensor_tensor(m.sp[:, i % 2], m.ps[:, q:q + 2, 0:432], m.za[:, i % 3], ALU.max).then_inc(s["b_sp"], 1)

    clamped(0)
    clamped(1)
    softplus(0)
    for i in range(8):
        if i + 1 < 8:
            softplus(i + 1)
        if i >= 1:
            head_output(i - 1)
        if i + 2 < 8:
            clamped(i + 2)
    head_output(7)
    residual(N_WO, 24)

    def mlp(layer, number, n_down, done):
        lo = first_token(number)
        norm(number, PC_NMLP + C * layer)
        for n in range(32):
            dve.wait_ge(s["chunk_act"], 32 * layer + n + 1)
            r = m.relu[:, n % 8, lo:TT]
            v.tensor_tensor(m.mlp[:, n, lo:TT], r, r, ALU.mult).then_inc(s["mlp_ready"], 1)
        residual(n_down, done, lo)

    mlp(0, 1, N_DOWN0, 32)

    lam = col(PC_LAM, C)
    link(v.tensor_scalar(m.lamc[:, 1, :], lam, -1.0, 0.0, ALU.mult, ALU.max))
    v.scalar_tensor_tensor(m.lamc[:, 0, :], lam, -1.0, lam, ALU.mult, ALU.max).then_inc(s["lam_in"], 1)
    link(v.memset(m.rec[:, :, 0:3], 0.0))
    dve.wait_ge(s["lam_out"], 1)
    link(v.tensor_tensor(m.lamc[:, 2, :], m.lamc[:, 0, :], m.lamc[:, 1, :], ALU.add))
    link(v.tensor_scalar(m.lamc[:, 3, :], m.lamc[:, 2, :], -8.0, None, ALU.mult))
    norm(2, PC_NMIX + C)
    def gate_input(n, number):
        dve.wait_ge(s["chunk_done"], number + 1)
        v.tensor_copy(m.gx[:, n, :], bank(number % 8)[:, 0:TT]).then_inc(s["chunk_dve"], 1)

    for c in range(C):
        dve.wait_ge(s["chunk_done"], N_LIN + c + 1)
        v.tensor_copy(m.rec[:, c, 3:3 + TT], bank(c)[:, 0:TT]).then_inc(s["chunk_dve"], 1)
        dve.wait_ge(s["chunk_dve"], 40 + c + 1)
        un = m.u[:, c, :]
        link(v.tensor_scalar(un, m.rec[:, c, 0:TT], col(PC_CONVW + c), col(PC_CONVB + c), ALU.mult, ALU.add))
        for q in range(1, 4):
            last = v.scalar_tensor_tensor(un, m.rec[:, c, q:q + TT], col(PC_CONVW + C * q + c), un,
                                          ALU.mult, ALU.add)
            if q < 3:
                link(last)
        last.then_inc(s["u_ready"], 1)
    for n in range(4):
        gate_input(n, N_LIN + C + n)
    for c in range(C):
        dve.wait_ge(s["r_ready"], c + 1)
        v.tensor_scalar(m.la[:, c, :], m.r[:, c, :], m.lamc[:, 3, c:c + 1], None, ALU.mult).then_inc(s["a_in"], 1)
    dve.wait_ge(s["r_ready"], 16)
    link(v.tensor_tensor(m.ig, m.ig, m.u, ALU.mult))
    dve.wait_ge(s["a_exp"], 2)
    link(v.tensor_tensor(m.r, m.am, m.am, ALU.mult))
    v.scalar_tensor_tensor(m.th, m.r, 1.0, m.th, ALU.add, ALU.mult).then_inc(s["mult_in"], 1)
    for n in range(4):
        gate_input(4 + n, N_LIN3 + n)
    dve.wait_ge(s["chunk_dve"], 56)
    x, x3 = m.gx[:, 4:8, :], m.g3[:, 4:8, :]
    link(v.tensor_tensor(x3, x, x, ALU.mult))
    link(v.tensor_scalar(x3, x3, GELU_A, 1.0, ALU.mult, ALU.add))
    v.tensor_tensor(x3, x3, x, ALU.mult).then_inc(s["gate_tanh_in2"], 1)
    dve.wait_ge(s["mult_root"], 1)
    link(v.tensor_tensor(m.ig, m.ig, m.th, ALU.mult))
    for h in range(2):
        dve.wait_ge(s["gate_tanh"], h + 1)
        half = slice(4 * h, 4 * h + 4)
        link(v.scalar_tensor_tensor(m.g3[:, half, :], m.g3[:, half, :], 1.0, m.gx[:, half, :], ALU.add, ALU.mult))
        for c in range(4 * h, 4 * h + 4):
            link(v.tensor_tensor_scan(m.hs[:, c, :], m.am[:, c, :], m.ig[:, c, :], 0.0, ALU.mult, ALU.add))
            v.scalar_tensor_tensor(m.hn[:, c, :], m.hs[:, c, :], 0.5, m.g3[:, c, :], ALU.mult,
                                   ALU.mult).then_inc(s["lru_y"], 1)
    residual(N_LOUT, 56, META)
    mlp(1, 3, N_DOWN1, 64)
    norm(4, PC_NFIN)
    for n in (0, 2):
        dve.wait_ge(s["final_turned"], n + 1)
        v.tensor_copy(m.out_tok[:, n // 2, 0:512], bank(n)).then_inc(s["out_ready_dve"], 1)


INPUTS = ["x", "c", "ada_w", "ada_b", "ln1_g", "ln2_g", "w_in", "nsa_q_gain", "nsa_k_gain", "nsa_cmp_pos",
          "nsa_cmp_w1", "nsa_cmp_w2", "moba_q_gain", "moba_k_gain", "w_out", "router_w", "router_b",
          "exp_w1", "exp_b1", "exp_w2", "exp_b2", "meta_tokens_2", "norm_mix_2", "norm_mlp_2",
          "sb_w_qkv_2", "sb_w_o_2", "lru_w_in_2", "lru_conv_w_2", "lru_conv_b_2", "lru_w_rg_2",
          "lru_b_rg_2", "lru_w_ig_2", "lru_b_ig_2", "lru_lambda_2", "lru_w_out_2", "mlp_w_up_2",
          "mlp_w_down_2", "norm_final_2"]


def build(nc, a, out):
    with ExitStack() as ctx:
        m = Memory(nc, ctx)
        s = Signals(nc, ctx)
        block = ctx.enter_context(nc.Block())

        @block.sync
        def _(sp):
            program_sync(nc, sp, m, s, a)
            for t in range(2):
                sp.wait_ge(s["out_ready_dve"], t + 1)
                sp.wait_ge(s["out_ready_act"], t + 1)
                sp.dma_start(out[0, P * t:P * t + P, :], m.out_tok[:, t, :]).then_inc(s["out_stored"], 16)
            sp.wait_ge(s["out_stored"], 32)

        @block.gpsimd
        def _(pool):
            program_gpsimd(nc, pool, m, s, a)

        @block.scalar
        def _(act):
            program_scalar(nc, act, m, s, a)

        @block.vector
        def _(dve):
            program_vector(nc, dve, m, s, a)

        @block.tensor
        def _(pe):
            program_tensor(nc, pe, m, s, a)


def kernel(**inputs):
    import concourse.bacc as bacc
    from concourse.bass_utils import run_bass_kernel_spmd

    nc = bacc.Bacc("TRN2", target_bir_lowering=False, num_devices=1)
    arrays, aps = {}, {}
    for name in INPUTS:
        value = np.ascontiguousarray(inputs[name])
        arrays[f"in_{name}"] = value
        aps[name] = nc.dram_tensor(f"in_{name}", value.shape, mybir.dt.from_np(value.dtype),
                                   kind="ExternalInput").ap()
    out = nc.dram_tensor("out", (1, T, D), F32, kind="ExternalOutput").ap()
    build(nc, aps, out)
    got = run_bass_kernel_spmd(nc, [arrays], core_ids=[0])
    return got.results[0]["out"]
```
